# Optimizing a Trainium2 kernel written in Bass

```python
import math
import jax, jax.numpy as jnp
from jax import lax
import numpy as np

D_MODEL = 1024
BATCH = 1
SEQ = 512
DEPTH = 2

HEAD_DIM = 64
N_Q_HEADS = 8
N_KV_HEADS = 2
GROUP = N_Q_HEADS // N_KV_HEADS
WINDOW = 128
ATTN_BLOCK = 128
ROPE_THETA = 500000.0
ROT_DIM = HEAD_DIM // 4
ATTN_WIDTH = N_Q_HEADS * HEAD_DIM
KV_WIDTH = N_KV_HEADS * HEAD_DIM

MLSTM_HEADS = 4
MLSTM_HEAD_DIM = D_MODEL // 8
MLSTM_WIDTH = MLSTM_HEADS * MLSTM_HEAD_DIM
MLSTM_CHUNK = 128

CONV_WIDTH = D_MODEL // 2
CONV_K = 3

N_BRANCH = 3
BRANCH_WIDTH = 512
D_FF = 2816
LN_EPS = 1e-5
ALPHA = (2.0 * DEPTH) ** 0.25
BETA = (8.0 * DEPTH) ** -0.25
NEG_INF = -1e30

SIZES = (ATTN_WIDTH, KV_WIDTH, KV_WIDTH,
         MLSTM_WIDTH, MLSTM_WIDTH, MLSTM_WIDTH, MLSTM_WIDTH, MLSTM_HEADS, MLSTM_HEADS,
         CONV_WIDTH, CONV_WIDTH, CONV_WIDTH,
         N_BRANCH * D_MODEL)
P_IN = sum(SIZES)

kernel_name = "hybrid_swa_mlstm_shortconv_macaron_deepnorm"

def _split_points():
    pts, acc = [], 0
    for s in SIZES[:-1]:
        acc += s
        pts.append(acc)
    return pts

def layer_norm(x, w, b):
    xf = x.astype(jnp.float32)
    mu = jnp.mean(xf, axis=-1, keepdims=True)
    xc = xf - mu
    var = jnp.mean(xc * xc, axis=-1, keepdims=True)
    y = xc * lax.rsqrt(var + LN_EPS) * w.astype(jnp.float32) + b.astype(jnp.float32)
    return y.astype(x.dtype)

def swiglu(x, w_gu, w_down):
    g, u = jnp.split(x @ w_gu, 2, axis=-1)
    return (jax.nn.silu(g) * u) @ w_down

def partial_rope(t, positions):
    half = ROT_DIM // 2
    inv_freq = ROPE_THETA ** (-jnp.arange(0, ROT_DIM, 2, dtype=jnp.float32) / ROT_DIM)
    ang = positions.astype(jnp.float32)[..., None] * inv_freq
    cos = jnp.cos(ang)[:, :, None, :].astype(t.dtype)
    sin = jnp.sin(ang)[:, :, None, :].astype(t.dtype)
    t1, t2, rest = t[..., :half], t[..., half:ROT_DIM], t[..., ROT_DIM:]
    return jnp.concatenate([t1 * cos - t2 * sin, t2 * cos + t1 * sin, rest], axis=-1)

def sliding_window_attention(q, k, v, sinks):
    B, S = q.shape[0], q.shape[1]
    L = ATTN_BLOCK
    nb = S // L
    qb = q.reshape(B, nb, L, N_KV_HEADS, GROUP, HEAD_DIM)
    kb = k.reshape(B, nb, L, N_KV_HEADS, HEAD_DIM)
    vb = v.reshape(B, nb, L, N_KV_HEADS, HEAD_DIM)
    zk = jnp.zeros_like(kb[:, :1])
    kk = jnp.concatenate([jnp.concatenate([zk, kb[:, :-1]], axis=1), kb], axis=2)
    vv = jnp.concatenate([jnp.concatenate([zk, vb[:, :-1]], axis=1), vb], axis=2)
    s = jnp.einsum('bnqhgd,bnkhd->bnhgqk', qb, kk,
                   preferred_element_type=jnp.float32) * (HEAD_DIM ** -0.5)
    qi = jnp.arange(L)[:, None]
    kj = jnp.arange(2 * L)[None, :]
    rel = qi + L - kj
    band = (rel >= 0) & (rel < WINDOW)
    valid = (jnp.arange(nb)[:, None, None] > 0) | (kj >= L)[None]
    mask = band[None] & valid
    s = jnp.where(mask[None, :, None, None], s, NEG_INF)
    sk = sinks.astype(jnp.float32).reshape(N_KV_HEADS, GROUP)[None, None, :, :, None, None]
    m = jnp.maximum(jnp.max(s, axis=-1, keepdims=True), sk)
    p = jnp.exp(s - m)
    p = p / (jnp.sum(p, axis=-1, keepdims=True) + jnp.exp(sk - m))
    o = jnp.einsum('bnhgqk,bnkhd->bnqhgd', p.astype(v.dtype), vv)
    return o.reshape(B, S, N_Q_HEADS * HEAD_DIM)

def mlstm_chunkwise(q, k, v, i_pre, f_pre):
    B, S, H, d = q.shape
    L = MLSTM_CHUNK
    nc = S // L
    f32 = jnp.float32

    def chunk4(t):
        return t.astype(f32).reshape(B, nc, L, H, d).transpose(1, 0, 3, 2, 4)

    def chunk3(t):
        return t.astype(f32).reshape(B, nc, L, H).transpose(1, 0, 3, 2)

    qc = chunk4(q)
    kc = chunk4(k) * (d ** -0.5)
    vc = chunk4(v)
    ic = chunk3(i_pre)
    fc = chunk3(jax.nn.log_sigmoid(f_pre.astype(f32)))
    causal = jnp.tril(jnp.ones((L, L), dtype=bool))

    def step(carry, xs):
        C, n, m = carry
        qt, kt, vt, it, ft = xs
        b = jnp.cumsum(ft, axis=-1)
        logw = b[..., :, None] - b[..., None, :] + it[..., None, :]
        logw = jnp.where(causal, logw, NEG_INF)
        inter = b + m[..., None]
        m_t = jnp.maximum(inter, jnp.max(logw, axis=-1))
        w_inter = jnp.exp(inter - m_t)
        scores = jnp.einsum('bhtd,bhsd->bhts', qt, kt) * jnp.exp(logw - m_t[..., None])
        num = w_inter[..., None] * jnp.einsum('bhtk,bhvk->bhtv', qt, C) + \
            jnp.einsum('bhts,bhsv->bhtv', scores, vt)
        den = w_inter * jnp.einsum('bhtk,bhk->bht', qt, n) + jnp.sum(scores, axis=-1)
        h = num / jnp.maximum(jnp.abs(den), jnp.exp(-m_t))[..., None]
        m_new = m_t[..., -1]
        bL = b[..., -1]
        decay = jnp.exp(bL + m - m_new)
        ws = jnp.exp(bL[..., None] - b + it - m_new[..., None])
        C_new = decay[..., None, None] * C + jnp.einsum('bhs,bhsv,bhsk->bhvk', ws, vt, kt)
        n_new = decay[..., None] * n + jnp.einsum('bhs,bhsk->bhk', ws, kt)
        return (C_new, n_new, m_new), h

    init = (jnp.zeros((B, H, d, d), f32), jnp.zeros((B, H, d), f32), jnp.zeros((B, H), f32))
    _, hs = lax.scan(step, init, (qc, kc, vc, ic, fc))
    return hs.transpose(1, 0, 3, 2, 4).reshape(B, S, H, d)

def short_gated_conv(xin, bg, cg, w):
    S = xin.shape[1]
    u = cg * xin
    up = jnp.pad(u, ((0, 0), (CONV_K - 1, 0), (0, 0)))
    y = w[0] * up[:, 0:S]
    for j in range(1, CONV_K):
        y = y + w[j] * up[:, j:j + S]
    return bg * y

def hybrid_mixer(x, positions, w_in, b_in, sinks, mlstm_norm_w, conv_w, w_branch, w_out):
    B, S, _ = x.shape
    proj = x @ w_in + b_in
    (aq, ak, av, mq, mk, mv, mo, mi, mf, cx, cb, cc, gates) = jnp.split(proj, _split_points(), axis=-1)
    aq = partial_rope(aq.reshape(B, S, N_Q_HEADS, HEAD_DIM), positions)
    ak = partial_rope(ak.reshape(B, S, N_KV_HEADS, HEAD_DIM), positions)
    av = av.reshape(B, S, N_KV_HEADS, HEAD_DIM)
    y_attn = sliding_window_attention(aq, ak, av, sinks)
    h = mlstm_chunkwise(mq.reshape(B, S, MLSTM_HEADS, MLSTM_HEAD_DIM),
                        mk.reshape(B, S, MLSTM_HEADS, MLSTM_HEAD_DIM),
                        mv.reshape(B, S, MLSTM_HEADS, MLSTM_HEAD_DIM), mi, mf)
    hm = jnp.mean(h, axis=-1, keepdims=True)
    hc = h - hm
    h = hc * lax.rsqrt(jnp.mean(hc * hc, axis=-1, keepdims=True) + LN_EPS)
    h = h.reshape(B, S, MLSTM_WIDTH) * mlstm_norm_w.astype(jnp.float32)
    y_mlstm = h.astype(x.dtype) * jax.nn.sigmoid(mo)
    y_conv = short_gated_conv(cx, cb, cc, conv_w)
    g = jax.nn.sigmoid(gates).reshape(B, S, N_BRANCH, D_MODEL)
    merged = (g[:, :, 0] * (y_attn @ w_branch[0]) +
              g[:, :, 1] * (y_mlstm @ w_branch[1]) +
              g[:, :, 2] * (y_conv @ w_branch[2]))
    return merged @ w_out

def setup_inputs(seed: int = 0) -> dict:
    key = jax.random.key(seed)
    ks = jax.random.split(key, 16)
    nrm = jax.random.normal
    x = nrm(ks[0], (BATCH, SEQ, D_MODEL), jnp.float32)
    positions = (jnp.arange(SEQ, dtype=jnp.int32)[None, :] +
                 jax.random.randint(ks[1], (BATCH, 1), 0, 1024, dtype=jnp.int32))
    w_in = nrm(ks[2], (DEPTH, D_MODEL, P_IN), jnp.float32) * D_MODEL ** -0.5
    b_in = nrm(ks[3], (DEPTH, P_IN), jnp.float32) * 0.02
    f_off = sum(SIZES[:8])
    b_in = b_in.at[:, f_off:f_off + MLSTM_HEADS].add(jnp.linspace(3.0, 6.0, MLSTM_HEADS, dtype=jnp.float32))
    attn_sinks = nrm(ks[4], (DEPTH, N_Q_HEADS), jnp.float32) * 0.5
    mlstm_norm_w = 1.0 + 0.02 * nrm(ks[5], (DEPTH, MLSTM_WIDTH), jnp.float32)
    conv_w = nrm(ks[6], (DEPTH, CONV_K, CONV_WIDTH), jnp.float32) * CONV_K ** -0.5
    w_branch = nrm(ks[7], (DEPTH, N_BRANCH, BRANCH_WIDTH, D_MODEL), jnp.float32) * (BRANCH_WIDTH ** -0.5 * BETA)
    w_out = nrm(ks[8], (DEPTH, D_MODEL, D_MODEL), jnp.float32) * (D_MODEL ** -0.5 * BETA)
    ffn1_w_gu = nrm(ks[9], (DEPTH, D_MODEL, 2 * D_FF), jnp.float32) * D_MODEL ** -0.5
    ffn1_w_down = nrm(ks[10], (DEPTH, D_FF, D_MODEL), jnp.float32) * (D_FF ** -0.5 * BETA)
    ffn2_w_gu = nrm(ks[11], (DEPTH, D_MODEL, 2 * D_FF), jnp.float32) * D_MODEL ** -0.5
    ffn2_w_down = nrm(ks[12], (DEPTH, D_FF, D_MODEL), jnp.float32) * (D_FF ** -0.5 * BETA)
    ln_w = 1.0 + 0.02 * nrm(ks[13], (DEPTH, 3, D_MODEL), jnp.float32)
    ln_b = 0.02 * nrm(ks[14], (DEPTH, 3, D_MODEL), jnp.float32)
    return {"x": x, "positions": positions, "w_in": w_in, "b_in": b_in,
            "attn_sinks": attn_sinks, "mlstm_norm_w": mlstm_norm_w, "conv_w": conv_w,
            "w_branch": w_branch, "w_out": w_out,
            "ffn1_w_gu": ffn1_w_gu, "ffn1_w_down": ffn1_w_down,
            "ffn2_w_gu": ffn2_w_gu, "ffn2_w_down": ffn2_w_down,
            "ln_w": ln_w, "ln_b": ln_b}

def reference(x, positions, w_in, b_in, attn_sinks, mlstm_norm_w, conv_w, w_branch, w_out,
              ffn1_w_gu, ffn1_w_down, ffn2_w_gu, ffn2_w_down, ln_w, ln_b):
    for l in range(DEPTH):
        x = layer_norm(ALPHA * x + 0.5 * swiglu(x, ffn1_w_gu[l], ffn1_w_down[l]), ln_w[l, 0], ln_b[l, 0])
        mix = hybrid_mixer(x, positions, w_in[l], b_in[l], attn_sinks[l], mlstm_norm_w[l],
                           conv_w[l], w_branch[l], w_out[l])
        x = layer_norm(ALPHA * x + mix, ln_w[l, 1], ln_b[l, 1])
        x = layer_norm(ALPHA * x + 0.5 * swiglu(x, ffn2_w_gu[l], ffn2_w_down[l]), ln_w[l, 2], ln_b[l, 2])
    return x


_drawn_inputs = setup_inputs


def setup_inputs(seed=0):
    import zlib

    import numpy as np

    out = dict(_drawn_inputs(seed))
    spreads = {}
    factors = {'attn_sinks': 51.794, 'mlstm_norm_w': 34.887}
    for name, (base, spread) in spreads.items():
        noise = np.random.default_rng([zlib.crc32(name.encode()), seed]).standard_normal(out[name].shape)
        drawn = base * np.exp(spread * noise) if base else spread * noise
        out[name] = __import__('jax').numpy.asarray(drawn.astype(out[name].dtype))
    for name, factor in factors.items():
        out[name] = (out[name] * factor).astype(out[name].dtype)
    return out
```

```python
from contextlib import ExitStack

import concourse.bass as bass
import numpy as np
from concourse import mybir

F32 = mybir.dt.float32
F32R = mybir.dt.float32r
I32 = mybir.dt.int32
ALU = mybir.AluOpType
ACT = mybir.ActivationFunctionType
AX = mybir.AxisListType

P = 128
SEQ, D, DEPTH = 512, 1024, 2
KD = D // P
DFF = 2816
KF = DFF // P
NB = SEQ // P
HD = 64
NQ, NKV = 8, 2
MH = 4
ROT = HD // 4
THETA = 500000.0
WB = 512
KB = WB // P
EPS = 1e-5
ALPHA = (2.0 * DEPTH) ** 0.25
NEG = -1e30
P_IN = 7432
TWO_PI = 2.0 * np.pi

C_AQ, C_AK, C_AV, C_MQ = 0, 512, 640, 768
C_MO, C_IF, C_CX = 2304, 2816, 2824
C_GATE = C_CX + 3 * WB
B_Q, B_K, B_V, B_MQ, B_MK, B_MV, B_MO, B_CX, B_CC, B_CB, B_G = 0, 4, 5, 6, 10, 14, 18, 22, 26, 30, 34
PAR_LN = 58
PAR_NW = PAR_LN + 48
PAR_CONV = PAR_NW + 4
PAR_IF = PAR_CONV + 12
PAR_SINK = PAR_IF + 8
NPAR = PAR_SINK + 8
K_ID, K_ONE, K_ROT, K_MASK, K_MT, K_FREQ = 0, 128, 256, 384, 640, 768
K_HM = 769
NCONST = K_HM + 16

S_FFN = KF + 12
S_MIX = 40
S_LAYER = 2 * S_FFN + S_MIX
OWN = {"scalar": 3, "vector": 179, "gpsimd": 27}
BRANCH_ORDER = (2, 0, 1)


def build(nc, xT, positions, w_in, w_branch, w_out, gu1, down1, gu2, down2, par_in, const_in, outT):
    ctx = ExitStack()
    with ctx:
        base = (nc.sbuf_base + 127) // 128 * 128
        top = [base]

        def at(name, shape, dt, offset):
            return nc.alloc_sbuf_tensor_at(name, shape, dt, offset=offset)

        def place(name, shape, dt=F32):
            size = int(np.prod(shape[1:])) * 4
            t = at(name, shape, dt, top[0])
            top[0] += (size + 31) // 32 * 32
            return t

        KB1 = 1024
        x_at = top[0]
        x = place("x", [P, KD, SEQ])
        xh = place("xh", [P, KD, SEQ], F32R)
        xl = place("xl", [P, KD, SEQ], F32R)
        raw = [place(f"raw{i}", [P, 2048]) for i in range(2)]
        wh = [place(f"wh{i}", [P, 2048], F32R) for i in range(2)]
        wl = [place(f"wl{i}", [P, 2048], F32R) for i in range(2)]
        big_at = top[0]
        hh = place("hh", [P, KF, SEQ], F32R)
        hl = place("hl", [P, KF, SEQ], F32R)

        def big(name, kb, shape, dt=F32):
            return at(name, shape, dt, big_at + int(kb * KB1))

        q = big("q", 0, [P, 4, SEQ])
        kT = big("kT", 8, [P, SEQ])
        vtok = big("vtok", 10, [P, NB, P])
        mq = big("mq", 12, [P, MH, SEQ])
        mk = big("mk", 20, [P, MH, SEQ])
        mv = big("mv", 28, [P, MH, SEQ])
        cx = big("cx", 36, [P, 4, SEQ])
        cc = big("cc", 44, [P, 4, SEQ])
        cb = big("cb", 52, [P, 4, SEQ])
        gt = big("gt", 68, [P, 4, SEQ])
        yA = big("yA", 76, [P, 4, SEQ])
        vT = big("vT", 84, [P, SEQ])
        mtmp = big("mtmp", 84, [P, SEQ])
        ropetmp = big("ropetmp", 86, [P, SEQ])
        convtmp = big("convtmp", 86, [P, SEQ])
        og = big("og", 44, [P, 4, SEQ])
        yCl = big("yCl", 0, [P, 4, SEQ], F32R)
        yCh = big("yCh", 60, [P, 4, SEQ], F32R)
        yAl = big("yAl", 0, [P, 4, SEQ], F32R)
        yAh = big("yAh", 60, [P, 4, SEQ], F32R)
        yMh = big("yMh", 36, [P, 4, SEQ], F32R)
        yMl = big("yMl", 52, [P, 4, SEQ], F32R)
        mh = [big(f"mh{i}", (12, 20)[i], [P, 4, SEQ], F32R) for i in range(2)]
        ml = [big(f"ml{i}", (28, 60)[i], [P, 4, SEQ], F32R) for i in range(2)]
        CS = big("CS", 8, [P, 3, P])
        ytmp = big("ytmp", 10, [P, SEQ])
        ln_d = big("ln_d", 68, [P, SEQ])
        ln_r = big("ln_r", 70, [P, SEQ])
        ln_s6 = big("ln_s6", 72, [P, SEQ])
        ln_s7 = big("ln_s7", 74, [P, SEQ])
        sx = [at(f"sx{i}", [P, 4, 256], F32, x_at + 4 * KB1 * i) for i in range(2)]
        pT = at("pT", [P, 2, SEQ], F32, x_at + 8 * KB1)

        const = place("const", [P, NCONST])
        cosT = place("cosT", [P, SEQ])
        sinT = place("sinT", [P, SEQ])
        par_all = place("par_all", [P, DEPTH, NPAR])
        par = place("par", [P, NPAR])
        kbias = place("kbias", [P, MH])
        NS = place("NS", [P, 3])
        cols = place("cols", [P, 5, 16])
        gi = place("gi", [P, 16])
        gf = place("gf", [P, 16])
        gs = place("gs", [P, 16])
        mx = place("mx", [P, 4])
        nmx = place("nmx", [P, 4])
        es = place("es", [P, 4])
        sums = place("sums", [P, 4])
        dn = place("dn", [P, 12])
        dens = place("dens", [P, 4])
        nden = place("nden", [P, 4])
        bst = place("bst", [P, 4, 6])
        bag = place("bag", [P, 4, 2])
        rst = place("rst", [P, 4])
        mrow = place("mrow", [1, 96])
        wif = place("wif", [P, KD, 8])
        t_at = top[0]

        def tmp(name, kb, shape, dt=F32):
            assert t_at + int(kb * KB1) + int(np.prod(shape[1:])) * 4 <= nc.sbuf_usable_end
            return at(name, shape, dt, t_at + int(kb * KB1))

        ln_S = tmp("ln_S", 0, [P, SEQ])
        ln_Q = tmp("ln_Q", 2, [P, SEQ])
        ln_C = tmp("ln_C", 4, [P, SEQ])
        ln_sq = [tmp(f"ln_sq{i}", 6 + 2 * i, [P, SEQ]) for i in range(2)]
        sil = [tmp(f"sil{i}", 2 * i, [P, SEQ]) for i in range(2)]
        hp = [tmp(f"hp{i}", 4 + 2 * i, [P, SEQ]) for i in range(2)]
        rf, ri, rb, ra, rloc, rg, rm, rz = (tmp(f"row{i}", 0.5 * i, [16, P]) for i in range(8))
        rowx = tmp("rowx", 4, [16, NB, P])
        Dm = tmp("Dm", 6, [P, NB, P])
        kw = tmp("kw", 8, [P, NB, P])
        vt = tmp("vt", 10, [P, NB, P])
        numh = big("numh", 86, [P, NB, P])
        ident = const[:, K_ID:K_ID + P]
        ones = const[:, K_ONE:K_ONE + P]

        pm = [ctx.enter_context(nc.psum_tensor(f"main{i}", [P, SEQ], F32)) for i in range(4)]
        sd = ctx.enter_context(nc.psum_tensor("side", [P, 4, SEQ], F32))

        class Signal:

            def __init__(self, name, per_layer, start=0):
                self.sem = ctx.enter_context(nc.semaphore(name))
                self.name, self.per, self.start = name, per_layer, start

            def val(self, layer, count):
                assert count + self.start > 0, self.name
                return layer * self.per + (count + self.start)

        class Order:

            def __init__(self, eng, own):
                self.eng, self.own = eng, own
                self.n, self.last, self.loop, self.layer = {}, None, None, 0

            def up(self, sig=None):
                sig = sig or self.own
                self.n[sig] = self.n.get(sig, 0) + 1
                self.last = sig
                return sig.sem, 1

            def settle(self):
                sig = self.last
                v = sig.val(self.layer, self.n[sig])
                if self.loop is not None:
                    i, per = self.loop
                    v = v + i * per[sig]
                self.eng.wait_ge(sig.sem, v)

            def enter(self, i, per):
                self.loop, self.was = (i, per), dict(self.n)

            def leave(self, times):
                i, per = self.loop
                for sig in self.n:
                    d = self.n[sig] - self.was.get(sig, 0)
                    assert d == per.get(sig, 0), (d, per.get(sig, 0))
                    self.n[sig] += d * (times - 1)
                self.loop = None

            def done(self):
                for sig, n in self.n.items():
                    assert n == sig.per, (sig.name, n, sig.per)

        own_act = Signal("own_act", OWN["scalar"])
        own_dve = Signal("own_dve", OWN["vector"])
        own_pool = Signal("own_pool", OWN["gpsimd"])
        raw_in = [[Signal(f"raw_in{s}{h}", 16 * (S_LAYER // 2 + 1)) for h in range(2)] for s in range(2)]
        wif_in = Signal("wif_in", 16)
        start_in = Signal("start_in", 0)
        x_in = Signal("x_in", 0)
        pos_in = Signal("pos_in", 0)
        out_done = Signal("out_done", 0)
        w_hi = Signal("w_hi", 2 * S_LAYER)
        w_lo = Signal("w_lo", 2 * S_LAYER, start=3)
        slab_done = Signal("slab_done", S_LAYER, start=1)
        passed = Signal("passed", 0)
        setup = Signal("setup", 0)
        table_ready = Signal("table_ready", 0)
        x_ready = Signal("x_ready", 3 * KD, start=KD)
        xhi_ready = Signal("xhi_ready", 3 * KD, start=KD)
        par_ready = Signal("par_ready", 1)
        silu_ready = Signal("silu_ready", 4 * 11, start=1)
        hid_f = Signal("hid_f", 4 * 11, start=1)
        hid_h = Signal("hid_h", 4 * 11)
        hid_l = Signal("hid_l", 4 * 11)
        z_ready = Signal("z_ready", 3 * KD)
        cen_ready = Signal("cen_ready", 3 * KD)
        scaled = Signal("scaled", 3 * KD)
        sum6 = Signal("sum6", 3)
        centre_ps = Signal("centre_ps", 3)
        centre = Signal("centre", 3)
        d_ready = Signal("d_ready", 3 * KD)
        sq_ready = Signal("sq_ready", 3 * KD)
        part_sums = Signal("part_sums", 3 * 5)
        stat_ps = Signal("stat_ps", 3 * 2)
        stat_d = Signal("stat_d", 3)
        stat_d2 = Signal("stat_d2", 3)
        var_ready = Signal("var_ready", 3)
        std_ready = Signal("std_ready", 3)
        norm_ready = Signal("norm_ready", 3 * KD)
        proj = Signal("proj", 34)
        gate_ps = Signal("gate_ps", 1, start=1)
        rot_ps = Signal("rot_ps", 5)
        rot_used = Signal("rot_used", 5)
        roped = Signal("roped", 5)
        kb_ready = Signal("kb_ready", 1)
        v_ps = Signal("v_ps", 1)
        v_ready = Signal("v_ready", 1)
        f_abs = Signal("f_abs", 1)
        f_exp = Signal("f_exp", 1)
        f_one = Signal("f_one", 1)
        f_ln = Signal("f_ln", 1)
        gates_tok = Signal("gates_tok", 1)
        gate_in = Signal("gate_in", 1)
        rows_ps = Signal("rows_ps", 1)
        rows_in = Signal("rows_in", 1)
        scans = Signal("scans", 1)
        ends_ps = Signal("ends_ps", 1)
        carry = Signal("carry", 1)
        carry_ps = Signal("carry_ps", 1)
        g_rows = Signal("g_rows", 1)
        decay_row = Signal("decay_row", 1)
        exp_rows = Signal("exp_rows", 1)
        cols_ps = Signal("cols_ps", 1)
        cols_ready = Signal("cols_ready", 1)
        sc_ps = Signal("sc_ps", 8)
        sc_max = Signal("sc_max", 8)
        sc_exp = Signal("sc_exp", 8)
        p_ready = Signal("p_ready", 8)
        pT_ps = Signal("pT_ps", 8)
        pT_act = Signal("pT_act", 6)
        pT_dve = Signal("pT_dve", 8)
        o_ps = Signal("o_ps", 8)
        o_used = Signal("o_used", 8)
        rowx_ready = Signal("rowx_ready", MH)
        m1_ps = Signal("m1_ps", MH)
        dm_ready = Signal("dm_ready", MH)
        dexp = Signal("dexp", MH)
        vt_ready = Signal("vt_ready", MH)
        s_ready = Signal("s_ready", MH)
        m2_ps = Signal("m2_ps", MH)
        numl_ready = Signal("numl_ready", MH)
        st_ready = Signal("st_ready", MH)
        m3_ps = Signal("m3_ps", MH)
        mvar = Signal("mvar", MH)
        mstd = Signal("mstd", MH)
        hn_ready = Signal("hn_ready", MH)
        m4_ps = Signal("m4_ps", MH)
        ym_ready = Signal("ym_ready", MH)
        ym_hi = Signal("ym_hi", MH)
        ym_lo = Signal("ym_lo", MH)
        conv_u = Signal("conv_u", 4)
        yc_f = Signal("yc_f", 4)
        yc_hi = Signal("yc_hi", 4)
        yc_lo = Signal("yc_lo", 4)
        ya_hi = Signal("ya_hi", 4)
        ya_lo = Signal("ya_lo", 4)
        sig_ready = Signal("sig_ready", 24)
        br_ps = Signal("br_ps", 18)
        prod = Signal("prod", 24)
        merged = Signal("merged", 8)
        mg_hi = Signal("mg_hi", 8)
        mg_lo = Signal("mg_lo", 8)

        def f32(a):
            return a.bitcast(F32)

        def slab_shape(n):
            if n < KF:
                return 8, 256
            if n < S_FFN:
                return (8, 8, 6)[(n - KF) % 3], 256
            if n < S_FFN + S_MIX:
                s = n - S_FFN
                if s in (2, 3):
                    return 8, 128
                if 18 <= s < 36 and (s - 18) % 3 == 2:
                    return 4, 512
                return 8, 256
            return slab_shape(n - S_FFN - S_MIX)

        def half(n, h):
            k, c = slab_shape(n)
            first = k // 2 if k != 6 else 4
            return (0, first * c) if h == 0 else (first * c, k * c)

        def apart(eng):
            eng.sem_inc(passed.sem, 1)

        def pieces(n, h):
            a, b = half(n, h)
            if n not in (S_FFN, S_FFN + 1):
                return [(lambda t: t[:, a:b], lambda t: t[:, a:b])]

            def read(j):
                return lambda t: t[:, a:b].rearrange("p (k b j c) -> p k j b c", b=2, j=2, c=HD)[:, :, j]

            def write(j):
                return lambda t: t[:, a:b].rearrange("p (k j b c) -> p k j b c", j=2, b=2, c=HD)[:, :, j]

            return [(read(j), write(j)) for j in range(2)]

        block = ctx.enter_context(nc.Block())

        @block.sync
        def _(sp):
            par_src = par_in.rearrange("l p n -> p l n")
            sp.dma_start(const[:, :], const_in).then_inc(start_in.sem, 16)
            sp.dma_start(par_all[:, :, :], par_src).then_inc(start_in.sem, 16)
            sp.dma_start(x[:, :, :], xT.rearrange("(k p) t -> p k t", p=P)).then_inc(x_in.sem, 16)
            sp.dma_start(mq[:, 0, :].bitcast(I32), positions[0, :].partition_broadcast(P)).then_inc(pos_in.sem, 16)

            def load(layer, n, slot, src, it=None, per=0, count=0):
                v = w_lo.val(layer, 2 * n - 2)
                sp.wait_ge(w_lo.sem, v if it is None else v + it * 2 * per)
                apart(sp)
                kk = src.shape[1]
                k0 = kk // 2 if kk != 6 else 4
                cols_ = int(np.prod(src.shape[2:]))
                for h, (a, b) in enumerate(((0, k0), (k0, kk))):
                    dst = raw[slot][:, a * cols_:b * cols_].rearrange("p (k c) -> p k c", c=cols_)
                    if len(src.shape) == 4:
                        for g in range(2):
                            sp.dma_start(dst[:, :, 128 * g:128 * g + 128], src[:, a:b, g]).then_inc(raw_in[slot][h].sem, 16)
                    else:
                        sp.dma_start(dst, src[:, a:b]).then_inc(raw_in[slot][h].sem, 16)

            def tiles(w, layer):
                return w[layer].rearrange("(k p) n -> p k n", p=P)

            def ffn(layer, n0, gu, down):
                wg, wd = tiles(gu, layer), tiles(down, layer)
                with sp.Fori(0, 11) as i:
                    for j in range(2):
                        src = wg[:, :, bass.ds(i * 256 + j * DFF, 256)]
                        load(layer, n0 + j, j, src, it=i, per=2)
                for p in range(4):
                    for t in range(3):
                        n = n0 + KF + 3 * p + t
                        src = wd[:, 8 * t:min(8 * t + 8, KF), 256 * p:256 * p + 256]
                        load(layer, n, n % 2, src)

            with sp.Fori(0, DEPTH) as layer:
                ffn(layer, 0, gu1, down1)
                wi, wo = tiles(w_in, layer), tiles(w_out, layer)
                sp.wait_ge(gate_ps.sem, gate_ps.val(layer, 0))
                apart(sp)
                sp.dma_start(wif[:, :, :], wi[:, :, C_IF:C_IF + 8]).then_inc(wif_in.sem, 16)
                for s in range(S_MIX):
                    n = S_FFN + s
                    if s < 2:
                        src = wi[:, :, 0:512].rearrange("p k (b c) -> p k b c", b=2)[:, :, :, 128 * s:128 * s + 128]
                    elif s < 4:
                        src = wi[:, :, C_AK + 128 * (s - 2):C_AK + 128 * (s - 1)]
                    elif s < 10:
                        src = wi[:, :, C_MQ + 256 * (s - 4):C_MQ + 256 * (s - 3)]
                    elif s < 18:
                        c = {0: C_CX, 1: C_CX + 2 * WB, 2: C_CX + WB, 3: C_MO}[(s - 10) // 2] + 256 * (s % 2)
                        src = wi[:, :, c:c + 256]
                    elif s < 36:
                        t, r = divmod(s - 18, 3)
                        br, quad = BRANCH_ORDER[t // 2], t % 2
                        if r < 2:
                            c = C_GATE + br * D + quad * 512 + r * 256
                            src = wi[:, :, c:c + 256]
                        else:
                            src = w_branch[layer][br].rearrange("(k p) n -> p k n", p=P)[:, :, quad * 512:quad * 512 + 512]
                    else:
                        src = wo[:, :, 256 * (s - 36):256 * (s - 35)]
                    load(layer, n, n % 2, src)
                ffn(layer, S_FFN + S_MIX, gu2, down2)
            for k in range(KD):
                sp.wait_ge(norm_ready.sem, norm_ready.val(DEPTH - 1, 2 * KD + k + 1))
                sp.dma_start(outT[P * k:P * (k + 1), :], x[:, k, :]).then_inc(out_done.sem, 16)
            sp.wait_ge(out_done.sem, 16 * KD)

        @block.scalar
        def _(act):
            o = Order(act, own_act)
            act.sem_inc(silu_ready.sem, 1)

            act.wait_ge(x_in.sem, 16)
            for k in range(KD):
                act.activation(xh[:, k, :], x[:, k, :], ACT.Copy).then_inc(xhi_ready.sem, 1)
            act.wait_ge(setup.sem, SETUP_STEPS)
            act.activation(sinT[:, :], mq[:, 0, :], ACT.Sin).then_inc(table_ready.sem, 1)
            act.activation(cosT[:, :], mq[:, 1, :], ACT.Sin).then_inc(table_ready.sem, 1)

            def split(layer, n, it=None, per=0):
                slot = n % 2
                if n > 0:
                    v = slab_done.val(layer, n - 1)
                    act.wait_ge(slab_done.sem, v if it is None else v + it * per)
                for h in range(2):
                    v = raw_in[slot][h].val(layer, 16 * (n // 2 + 1 + (n >= S_FFN)))
                    act.wait_ge(raw_in[slot][h].sem, v if it is None else v + it * 16 * (per // 2))
                    for get, put in pieces(n, h):
                        ins = act.activation(put(wh[slot]), get(raw[slot]), ACT.Copy)
                    ins.then_inc(*o.up(w_hi))

            def centre_copy(layer, j):
                act.wait_ge(centre_ps.sem, centre_ps.val(layer, j + 1))
                act.activation(ln_C[:, :], sd[:, 0, :], ACT.Copy, scale=1.0 / (6 * P)).then_inc(*o.up(centre))

            def squares(layer, j, m):
                act.wait_ge(d_ready.sem, d_ready.val(layer, KD * j + m + 1))
                if 2 <= m < 6:
                    act.wait_ge(part_sums.sem, part_sums.val(layer, 5 * j + max(1, m - 2)))
                dst = ln_sq[m % 2] if m < 6 else (ln_s6, ln_s7)[m - 6]
                act.activation(dst[:, :], x[:, m, :], ACT.Square).then_inc(*o.up(sq_ready))

            def norm_tail(layer, j):
                squares(layer, j, 6)
                squares(layer, j, 7)
                act.wait_ge(stat_ps.sem, stat_ps.val(layer, 2 * j + 1))
                act.activation(ln_d[:, :], sd[:, 0, :], ACT.Copy, scale=1.0 / D).then_inc(*o.up(stat_d))
                o.settle()
                act.activation(ln_S[:, :], ln_d[:, :], ACT.Square).then_inc(*o.up(stat_d2))
                act.wait_ge(var_ready.sem, var_ready.val(layer, j + 1))
                act.activation(ln_Q[:, :], ln_r[:, :], ACT.Sqrt).then_inc(*o.up(std_ready))
                c = PAR_LN + 16 * j
                for m in range(KD):
                    act.wait_ge(scaled.sem, scaled.val(layer, KD * j + m + 1))
                    act.activation(x[:, m, :], x[:, m, :], ACT.Identity, bias=par[:, c + 8 + m:c + 9 + m],
                                   scale=par[:, c + m:c + m + 1]).then_inc(*o.up(norm_ready))
                    o.settle()
                    act.activation(xh[:, m, :], x[:, m, :], ACT.Copy).then_inc(*o.up(xhi_ready))

            def ffn(layer, n0, f):
                with act.Fori(0, 11) as i:
                    o.enter(i, {w_hi: 4, silu_ready: 2, hid_h: 2})
                    split(layer, n0 + 1, it=i, per=2)
                    split(layer, n0 + 2, it=i, per=2)
                    act.wait_ge(slab_done.sem, slab_done.val(layer, n0 + 1) + i * 2)
                    act.wait_ge(hid_f.sem, hid_f.val(layer, 22 * f) + i * 2)
                    act.activation(sil[0][:, :], pm[0][:, :], ACT.Silu).then_inc(*o.up(silu_ready))
                    act.activation(sil[1][:, :], pm[1][:, :], ACT.Silu).then_inc(*o.up(silu_ready))
                    for m in range(2):
                        act.wait_ge(hid_f.sem, hid_f.val(layer, 22 * f + m + 1) + i * 2)
                        act.activation(hh[:, bass.ds(i * 2 + m, 1), :], hp[m][:, :].unsqueeze(1), ACT.Copy).then_inc(*o.up(hid_h))
                    o.leave(11)
                for p in range(4):
                    for t in range(3):
                        n = n0 + KF + 3 * p + t
                        if n + 1 < S_LAYER:
                            split(layer, n + 1)
                        if p == 3 and t == 0:
                            centre_copy(layer, 2 * f)
                        if p == 3:
                            squares(layer, 2 * f, 2 * t)
                            squares(layer, 2 * f, 2 * t + 1)
                norm_tail(layer, 2 * f)

            def evacuate(layer, s):
                n = S_FFN + s
                par_ = n % 2
                act.wait_ge(slab_done.sem, slab_done.val(layer, n + 1))
                if s < 2:
                    outs = [(q[:, 2 * s + m, :], B_Q + 2 * s + m) for m in range(2)]
                elif s == 2:
                    outs = [(kT[:, :], B_K)]
                elif s == 3:
                    outs = [(vT[:, :], B_V)]
                elif s < 10:
                    dst = (mq, mk, mv)[(s - 4) // 2]
                    outs = [(dst[:, 2 * (s % 2) + m, :], B_MQ + 2 * (s - 4) + m) for m in range(2)]
                elif s < 18:
                    g = (s - 10) // 2
                    dst, b0 = ((cx, B_CX), (cc, B_CC), (cb, B_CB), (og, B_MO))[g]
                    outs = [(dst[:, 2 * (s % 2) + m, :], b0 + 2 * (s % 2) + m) for m in range(2)]
                if s == 16:
                    act.wait_ge(conv_u.sem, conv_u.val(layer, 4))
                for m, (dst, b) in enumerate(outs):
                    src = pm[2 * par_ + m][:, :]
                    if 6 <= s < 8:
                        act.activation(dst, src, ACT.Identity, bias=kbias[:, b - B_MK:b - B_MK + 1],
                                       scale=float(P) ** -0.5).then_inc(*o.up(proj))
                    else:
                        fn = ACT.Sigmoid if s >= 16 else ACT.Identity
                        act.activation(dst, src, fn, bias=par[:, b:b + 1]).then_inc(*o.up(proj))

            def memory_gates(layer, s):
                if s == 0:
                    act.wait_ge(gate_in.sem, gate_in.val(layer, 1))
                    act.activation(gs[:, :], gf[:, :], ACT.Abs).then_inc(*o.up(f_abs))
                    o.settle()
                    act.activation(gs[:, :], gs[:, :], ACT.Exp, scale=-1.0).then_inc(*o.up(f_exp))
                    act.wait_ge(f_one.sem, f_one.val(layer, 1))
                    act.activation(gs[:, :], gs[:, :], ACT.Ln).then_inc(*o.up(f_ln))
                if s == 4:
                    act.wait_ge(decay_row.sem, decay_row.val(layer, 1))
                    act.activation(mrow[0:1, 80:96], mrow[0:1, 64:80], ACT.Exp).then_inc(*o.up())
                    act.wait_ge(g_rows.sem, g_rows.val(layer, 1))
                    act.activation(rf[:, :], rg[:, :], ACT.Exp, bias=rz[:, 0:1], scale=-1.0).then_inc(*o.up())
                    act.activation(ri[:, :], rm[:, :], ACT.Exp, scale=-1.0).then_inc(*o.up())
                    act.activation(rb[:, :], ra[:, :], ACT.Exp, bias=rz[:, 1:2]).then_inc(*o.up(exp_rows))

            def attn_exp(layer, u):
                b = sx[u % 2]
                k0 = 128 if u < 2 else 0
                act.wait_ge(sc_max.sem, sc_max.val(layer, u + 1))
                for j in range(4):
                    act.activation(b[:, j, k0:256], b[:, j, k0:256], ACT.Exp, bias=nmx[:, j:j + 1],
                                   accum_out=sums[:, j:j + 1])
                act.activation(es[:, :], es[:, :], ACT.Exp).then_inc(*o.up(sc_exp))

            def attn_pT(layer, u):
                if u >= 2:
                    act.wait_ge(pT_ps.sem, pT_ps.val(layer, u + 1))
                    act.activation(pT[:, 0, :], sd[:, 2, :], ACT.Copy).then_inc(*o.up(pT_act))

            def attn_out(layer, u):
                blk, g = divmod(u, 2)
                act.wait_ge(o_ps.sem, o_ps.val(layer, u + 1))
                act.activation(yA[:, 2 * g:2 * g + 2, P * blk:P * blk + P],
                               sd[:, 2, 0:256].rearrange("p (a t) -> p a t", a=2), ACT.Copy).then_inc(*o.up(o_used))

            def mem1(layer, h):
                act.wait_ge(m1_ps.sem, m1_ps.val(layer, h + 1))
                act.activation(vt[:, :, :], sd[:, 3, :].rearrange("p (n t) -> p n t", n=NB), ACT.Copy).then_inc(*o.up(vt_ready))
                act.wait_ge(dm_ready.sem, dm_ready.val(layer, h + 1))
                for n in range(NB):
                    c = 4 * n + h
                    ins = act.activation(Dm[:, n, :], Dm[:, n, :], ACT.Exp, bias=cols[:, 0, c:c + 1])
                ins.then_inc(*o.up(dexp))

            def mem2(layer, h):
                act.wait_ge(m2_ps.sem, m2_ps.val(layer, h + 1))
                act.activation(numh[:, :, :], sd[:, 1, :].rearrange("p (n t) -> p n t", n=NB), ACT.Copy).then_inc(*o.up(numl_ready))

            def mem3(layer, h):
                act.wait_ge(mvar.sem, mvar.val(layer, h + 1))
                act.activation(rst[:, :], rst[:, :], ACT.Sqrt).then_inc(*o.up(mstd))

            def mem4(layer, h):
                act.wait_ge(ym_ready.sem, ym_ready.val(layer, h + 1))
                act.activation(yMh[:, h, :], ytmp[:, :], ACT.Copy).then_inc(*o.up(ym_hi))

            def mixer(layer):
                for s in range(S_MIX):
                    n = S_FFN + s
                    split(layer, n + 1)
                    if 6 <= s < 14:
                        attn_pT(layer, s - 6)
                    if s >= 18 and s < 30:
                        h, r = divmod(s - 18, 3)
                        if r == 0:
                            mem1(layer, h)
                        if r == 1:
                            mem3(layer, h)
                        if r == 2:
                            mem4(layer, h)
                    if s < 18:
                        evacuate(layer, s)
                    elif s < 36:
                        t, r = divmod(s - 18, 3)
                        if r < 2:
                            act.wait_ge(slab_done.sem, slab_done.val(layer, n + 1))
                            for m in range(2):
                                b = B_G + 8 * BRANCH_ORDER[t // 2] + 4 * (t % 2) + 2 * r + m
                                if t > 0:
                                    act.wait_ge(prod.sem, prod.val(layer, 4 * (t - 1) + 2 * r + m + 1))
                                act.activation(gt[:, 2 * r + m, :], pm[2 * r + m][:, :], ACT.Sigmoid,
                                               bias=par[:, b:b + 1]).then_inc(*o.up(sig_ready))
                        elif t >= 4:
                            for m in range(4):
                                k = 4 * (t - 4) + m
                                act.wait_ge(merged.sem, merged.val(layer, k + 1))
                                act.activation(mh[k // 4][:, k % 4, :], x[:, k, :], ACT.Copy).then_inc(*o.up(mg_hi))
                    if s in (0, 4):
                        memory_gates(layer, s)
                    if 6 <= s < 14:
                        attn_out(layer, s - 6)
                    if 5 <= s < 13:
                        attn_exp(layer, s - 5)
                    if s in (15, 16):
                        for c in (2 * (s - 15), 2 * (s - 15) + 1):
                            act.wait_ge(yc_f.sem, yc_f.val(layer, c + 1))
                            act.activation(yCh[:, c, :], convtmp[:, :], ACT.Copy).then_inc(*o.up(yc_hi))
                    if s == 23:
                        act.wait_ge(slab_done.sem, slab_done.val(layer, n + 1))
                        for c in range(4):
                            act.activation(yAh[:, c, :], yA[:, c, :], ACT.Copy).then_inc(*o.up(ya_hi))
                    if s >= 18 and s < 30 and (s - 18) % 3 == 0:
                        mem2(layer, (s - 18) // 3)
                    if s == 39:
                        centre_copy(layer, 1)
                        for m in range(6):
                            squares(layer, 1, m)
                norm_tail(layer, 1)

            with act.Fori(0, DEPTH) as layer:
                o.layer = layer
                act.wait_ge(kb_ready.sem, kb_ready.val(layer, 1))
                split(layer, 0)
                ffn(layer, 0, 0)
                mixer(layer)
                ffn(layer, S_FFN + S_MIX, 1)
                o.done()

        @block.gpsimd
        def _(pool):
            o = Order(pool, own_pool)

            def norm(layer, j):
                S, Q = ln_S[:, :], ln_Q[:, :]
                for m in range(1, 6):
                    pool.wait_ge(z_ready.sem, z_ready.val(layer, KD * j + m + 1))
                    first = x[:, 0, :] if m == 1 else S
                    nc.gpsimd.tensor_tensor(S, first, x[:, m, :], ALU.add).then_inc(*o.up(sum6 if m == 5 else None))
                    if m < 5:
                        o.settle()
                pool.wait_ge(centre_ps.sem, centre_ps.val(layer, j + 1))
                for m in range(1, 6):
                    pool.wait_ge(sq_ready.sem, sq_ready.val(layer, KD * j + m + 1))
                    first = (x[:, 0, :], ln_sq[0][:, :]) if m == 1 else (S, Q)
                    nc.gpsimd.tensor_tensor(S, first[0], x[:, m, :], ALU.add).then_inc(*o.up())
                    nc.gpsimd.tensor_tensor(Q, first[1], ln_sq[m % 2][:, :], ALU.add).then_inc(*o.up(part_sums))
                    o.settle()
                pool.wait_ge(stat_d.sem, stat_d.val(layer, j + 1))
                for m in range(KD):
                    nc.gpsimd.tensor_tensor(x[:, m, :], x[:, m, :], ln_d[:, :], ALU.subtract).then_inc(*o.up(cen_ready))

            with pool.Fori(0, DEPTH) as layer:
                o.layer = layer
                for j in range(3):
                    norm(layer, j)
                o.done()

        @block.vector
        def _(dve):
            o = Order(dve, own_dve)
            V = nc.vector
            steps = [0]

            def step(ins):
                ins.then_inc(setup.sem, 1)
                steps[0] += 1
                dve.wait_ge(setup.sem, steps[0])

            for t, sig in ((kbias, w_lo), (NS, w_lo), (mx, w_lo), (nmx, hid_f)):
                V.memset(t[:, :], 0.0).then_inc(sig.sem, 1)
            dve.wait_ge(x_in.sem, 16)
            for k in range(KD):
                dve.wait_ge(xhi_ready.sem, k + 1)
                V.tensor_tensor(xl[:, k, :], x[:, k, :], f32(xh[:, k, :]), ALU.subtract).then_inc(x_ready.sem, 1)
            dve.wait_ge(start_in.sem, 32)
            dve.wait_ge(pos_in.sem, 16)
            an, tu, co = mq[:, 0, :], mq[:, 1, :], mq[:, 2, :]
            step(V.tensor_copy(co, an.bitcast(I32)))
            step(V.tensor_scalar(an, co, const[:, K_FREQ:K_FREQ + 1], None, ALU.mult))
            step(V.tensor_scalar(tu, an, 1.0 / TWO_PI, None, ALU.mult))
            step(V.tensor_scalar(tu, tu, 12582912.0, None, ALU.add))
            step(V.tensor_scalar(tu, tu, -12582912.0, None, ALU.add))
            c1 = 6.28125
            c2 = float(np.float32(np.floor((TWO_PI - c1) * 2**20) / 2**20))
            for c in (c1, c2, TWO_PI - c1 - c2):
                step(V.scalar_tensor_tensor(out=an, in0=tu, scalar=-c, in1=an, op0=ALU.mult, op1=ALU.add))
            step(V.tensor_scalar(an, an, 3.1415925, -3.1415925, ALU.min, ALU.max))
            step(V.scalar_tensor_tensor(out=tu, in0=an, scalar=-1.0, in1=an, op0=ALU.mult, op1=ALU.max))
            step(V.tensor_scalar(tu, tu, -1.0, float(np.pi / 2), ALU.mult, ALU.add))
            assert steps[0] == SETUP_STEPS

            def split(layer, n, it=None, per=0):
                slot = n % 2
                for h in range(2):
                    v = w_hi.val(layer, 2 * n + h + 1)
                    dve.wait_ge(w_hi.sem, v if it is None else v + it * 2 * per)
                    for get, put in pieces(n, h):
                        ins = V.tensor_tensor(put(wl[slot]), get(raw[slot]), f32(put(wh[slot])), ALU.subtract)
                    ins.then_inc(*o.up(w_lo))

            def centred(layer, j, m):
                if m == 0:
                    dve.wait_ge(centre.sem, centre.val(layer, j + 1))
                V.tensor_tensor(x[:, m, :], x[:, m, :], ln_C[:, :], ALU.subtract).then_inc(*o.up(d_ready))

            def residual(layer, j, m, bank):
                if j != 1:
                    V.scalar_tensor_tensor(out=x[:, m, :], in0=x[:, m, :], scalar=ALPHA, in1=pm[bank][:, :],
                                           op0=ALU.mult, op1=ALU.add).then_inc(*o.up(z_ready))
                else:
                    V.scalar_tensor_tensor(out=x[:, m, :], in0=f32(xh[:, m, :]), scalar=ALPHA, in1=pm[bank][:, :],
                                           op0=ALU.mult, op1=ALU.add).then_inc(*o.up())
                    o.settle()
                    V.scalar_tensor_tensor(out=x[:, m, :], in0=f32(xl[:, m, :]), scalar=ALPHA, in1=x[:, m, :],
                                           op0=ALU.mult, op1=ALU.add).then_inc(*o.up(z_ready))

            def norm_tail(layer, j):
                for m in (6, 7):
                    o.settle()
                    centred(layer, j, m)
                dve.wait_ge(stat_ps.sem, stat_ps.val(layer, 2 * j + 2))
                dve.wait_ge(stat_d2.sem, stat_d2.val(layer, j + 1))
                V.scalar_tensor_tensor(out=ln_r[:, :], in0=sd[:, 1, :], scalar=1.0 / D, in1=ln_S[:, :],
                                       op0=ALU.mult, op1=ALU.subtract).then_inc(*o.up())
                o.settle()
                V.tensor_scalar(ln_r[:, :], ln_r[:, :], 0.0, EPS, ALU.max, ALU.add).then_inc(*o.up(var_ready))
                dve.wait_ge(std_ready.sem, std_ready.val(layer, j + 1))
                V.reciprocal(ln_r[:, :], ln_Q[:, :]).then_inc(*o.up())
                o.settle()

                def low(m):
                    dve.wait_ge(xhi_ready.sem, xhi_ready.val(layer, KD * j + m + 1))
                    V.tensor_tensor(xl[:, m, :], x[:, m, :], f32(xh[:, m, :]), ALU.subtract).then_inc(*o.up(x_ready))

                for m in range(KD):
                    dve.wait_ge(cen_ready.sem, cen_ready.val(layer, KD * j + m + 1))
                    V.tensor_tensor(x[:, m, :], x[:, m, :], ln_r[:, :], ALU.mult).then_inc(*o.up(scaled))
                    if m:
                        low(m - 1)
                low(KD - 1)

            def ffn(layer, n0, f):
                with dve.Fori(0, 11) as i:
                    o.enter(i, {w_lo: 4, hid_f: 2, hid_l: 2})
                    split(layer, n0 + 1, it=i, per=2)
                    split(layer, n0 + 2, it=i, per=2)
                    dve.wait_ge(slab_done.sem, slab_done.val(layer, n0 + 2) + i * 2)
                    for m in range(2):
                        dve.wait_ge(silu_ready.sem, silu_ready.val(layer, 22 * f + m + 1) + i * 2)
                        V.scalar_tensor_tensor(out=hp[m][:, :], in0=pm[2 + m][:, :], scalar=0.5, in1=sil[m][:, :],
                                               op0=ALU.mult, op1=ALU.mult).then_inc(*o.up(hid_f))
                    for m in range(2):
                        dve.wait_ge(hid_h.sem, hid_h.val(layer, 22 * f + m + 1) + i * 2)
                        c = bass.ds(i * 2 + m, 1)
                        V.tensor_tensor(hl[:, c, :], hp[m][:, :].unsqueeze(1), f32(hh[:, c, :]),
                                        ALU.subtract).then_inc(*o.up(hid_l))
                    o.leave(11)
                for p in range(4):
                    for t in range(3):
                        n = n0 + KF + 3 * p + t
                        if n + 1 < S_LAYER:
                            split(layer, n + 1)
                        if p == 3:
                            for m in (2 * t, 2 * t + 1):
                                centred(layer, 2 * f, m)
                    dve.wait_ge(slab_done.sem, slab_done.val(layer, n + 1))
                    for m in range(2):
                        residual(layer, 2 * f, 2 * p + m, 2 * (p % 2) + m)
                norm_tail(layer, 2 * f)

            def rope(layer, r, t, bank):
                dve.wait_ge(rot_ps.sem, rot_ps.val(layer, r + 1))
                V.tensor_tensor(ropetmp[:, :], sd[:, bank, :], sinT[:, :], ALU.mult).then_inc(*o.up(rot_used))
                V.tensor_tensor(t, t, cosT[:, :], ALU.mult).then_inc(*o.up())
                o.settle()
                V.tensor_tensor(t, t, ropetmp[:, :], ALU.add).then_inc(*o.up(roped))
                o.settle()

            def memory_gates(layer, s):
                if s == 0:
                    dve.wait_ge(gate_ps.sem, gate_ps.val(layer, 1))
                    g = sd[:, 3, 0:32].rearrange("p (n g) -> p n g", g=8)
                    for dst, c in ((gi, 0), (gf, 4)):
                        bias = par[:, PAR_IF + c:PAR_IF + c + 4].unsqueeze(1).broadcast_to([P, NB, 4])
                        ins = V.tensor_tensor(dst[:, :].rearrange("p (n h) -> p n h", h=4), g[:, :, c:c + 4], bias, ALU.add)
                    ins.then_inc(*o.up(gate_in))
                    dve.wait_ge(f_exp.sem, f_exp.val(layer, 1))
                    V.tensor_scalar(gs[:, :], gs[:, :], 1.0, None, ALU.add).then_inc(*o.up(f_one))
                    dve.wait_ge(f_ln.sem, f_ln.val(layer, 1))
                    V.scalar_tensor_tensor(out=gf[:, :], in0=gf[:, :], scalar=0.0, in1=gs[:, :],
                                           op0=ALU.min, op1=ALU.subtract).then_inc(*o.up(gates_tok))
                if s == 2:
                    dve.wait_ge(rows_ps.sem, rows_ps.val(layer, 1))
                    V.tensor_copy(rf[:, :], sd[0:16, 2, 0:128])
                    V.tensor_copy(ri[:, :], sd[0:16, 2, 128:256])
                    V.memset(rz[:, :], 0.0).then_inc(*o.up())
                    o.settle()
                    V.tensor_tensor_scan(rb[:, :], rf[:, :], rz[:, :], 0.0, ALU.add, ALU.add).then_inc(*o.up())
                    o.settle()
                    V.tensor_tensor(ra[:, :], ri[:, :], rb[:, :], ALU.subtract).then_inc(*o.up())
                    o.settle()
                    V.tensor_tensor_scan(rloc[:, :], ra[:, :], ra[:, :], -3e38, ALU.max, ALU.max).then_inc(*o.up(scans))
                if s == 3:
                    dve.wait_ge(ends_ps.sem, ends_ps.val(layer, 1))
                    V.tensor_copy(mrow[0:1, 0:32], sd[0:1, 2, 256:288])
                    V.memset(mrow[0:1, 32:36], 0.0).then_inc(*o.up())
                    for n in range(NB):
                        o.settle()
                        a, b, m, g = (mrow[0:1, c + 4 * n:c + 4 * n + 4] for c in (16, 0, 32, 48))
                        V.tensor_tensor(g, m, a, ALU.max).then_inc(*o.up(carry if n == NB - 1 else None))
                        o.settle()
                        if n < NB - 1:
                            V.tensor_tensor(mrow[0:1, 36 + 4 * n:40 + 4 * n], b, g, ALU.add).then_inc(*o.up())
                    V.tensor_tensor(mrow[0:1, 64:80], mrow[0:1, 32:48], mrow[0:1, 48:64], ALU.subtract).then_inc(*o.up(decay_row))
                if s == 4:
                    dve.wait_ge(carry_ps.sem, carry_ps.val(layer, 1))
                    V.tensor_copy(rz[:, 0:1], sd[0:16, 2, 300:301])
                    V.tensor_scalar(rz[:, 1:2], sd[0:16, 2, 301:302], -1.0, None, ALU.mult).then_inc(*o.up())
                    o.settle()
                    V.tensor_scalar(rg[:, :], rloc[:, :], rz[:, 0:1], None, ALU.max).then_inc(*o.up())
                    o.settle()
                    V.tensor_tensor(rm[:, :], rb[:, :], rg[:, :], ALU.add).then_inc(*o.up(g_rows))
                if s == 5:
                    dve.wait_ge(cols_ps.sem, cols_ps.val(layer, 1))
                    V.tensor_copy(cols[:, :, :], sd[:, 3, 0:80].rearrange("p (a b) -> p a b", a=5)).then_inc(*o.up(cols_ready))

            def attn_scores(layer, u):
                b, g = sx[u % 2], u % 2
                k0 = 128 if u < 2 else 0
                dve.wait_ge(sc_ps.sem, sc_ps.val(layer, u + 1))
                s4 = sd[:, 0:2, :].rearrange("p b (j k) -> p (b j) k", j=2)
                mask = const[:, K_MASK + k0:K_MASK + 256].unsqueeze(1).broadcast_to([P, 4, 256 - k0])
                V.scalar_tensor_tensor(out=b[:, :, k0:256], in0=s4[:, :, k0:256], scalar=float(HD) ** -0.5,
                                       in1=mask, op0=ALU.mult, op1=ALU.add).then_inc(*o.up())
                o.settle()
                V.tensor_reduce(mx[:, :], b[:, :, k0:256], AX.X, ALU.max).then_inc(*o.up())
                o.settle()
                sink = par[:, PAR_SINK + 4 * g:PAR_SINK + 4 * g + 4]
                V.tensor_tensor(mx[:, :], mx[:, :], sink, ALU.max).then_inc(*o.up())
                o.settle()
                V.tensor_tensor(es[:, :], sink, mx[:, :], ALU.subtract)
                V.tensor_scalar(nmx[:, :], mx[:, :], -1.0, None, ALU.mult).then_inc(*o.up(sc_max))

            def attn_norm(layer, u):
                b = sx[u % 2]
                k0 = 128 if u < 2 else 0
                dve.wait_ge(sc_exp.sem, sc_exp.val(layer, u + 1))
                V.tensor_tensor(sums[:, :], sums[:, :], es[:, :], ALU.add).then_inc(*o.up())
                o.settle()
                V.reciprocal(mx[:, :], sums[:, :]).then_inc(*o.up())
                o.settle()
                V.tensor_tensor(b[:, :, k0:256], b[:, :, k0:256], mx[:, :].unsqueeze(2).broadcast_to([P, 4, 256 - k0]),
                                ALU.mult).then_inc(*o.up(p_ready))

            def attn_pT(layer, u):
                dve.wait_ge(pT_ps.sem, pT_ps.val(layer, u + 1))
                V.tensor_copy(pT[:, 1, :], sd[:, 3, :]).then_inc(*o.up(pT_dve))

            def row_of(layer, h):
                hm = const[0:16, K_HM + 4 * h:K_HM + 4 * h + 4].unsqueeze(2).broadcast_to([16, NB, P])
                V.tensor_tensor(rowx[:, :, :], rg[:, :].unsqueeze(1).broadcast_to([16, NB, P]), hm,
                                ALU.mult).then_inc(*o.up(rowx_ready))

            def of_head(kind, h):
                return cols[:, kind, :].rearrange("p (n h) -> p n h", h=4)[:, :, h]

            def n4(a):
                return a.rearrange("p (n t) -> p n t", n=NB)

            def mem1(layer, h):
                dve.wait_ge(m1_ps.sem, m1_ps.val(layer, h + 1))
                mt = const[:, K_MT:K_MT + P].unsqueeze(1).broadcast_to([P, NB, P])
                V.scalar_tensor_tensor(out=Dm[:, :, :], in0=n4(sd[:, 1, :]), scalar=-1.0, in1=mt,
                                       op0=ALU.mult, op1=ALU.add).then_inc(*o.up(dm_ready))
                V.tensor_tensor(kw[:, :, :], n4(sd[:, 2, :]), of_head(3, h).unsqueeze(2).broadcast_to([P, NB, P]),
                                ALU.mult).then_inc(*o.up())
                dve.wait_ge(dexp.sem, dexp.val(layer, h + 1))
                V.tensor_tensor(Dm[:, :, :], Dm[:, :, :], n4(sd[:, 0, :]), ALU.mult).then_inc(*o.up(s_ready))

            def mem2(layer, h):
                dve.wait_ge(m2_ps.sem, m2_ps.val(layer, h + 1))
                V.tensor_copy(CS[:, 0, :], sd[:, 2, 0:P])
                V.tensor_copy(NS[:, 0:1], sd[:, 3, 8:9]).then_inc(*o.up())
                for n in (1, 2):
                    o.settle()
                    dec = cols[:, 4, 4 * n + h:4 * n + h + 1]
                    V.scalar_tensor_tensor(out=CS[:, n, :], in0=CS[:, n - 1, :], scalar=dec,
                                           in1=sd[:, 2, P * n:P * n + P], op0=ALU.mult, op1=ALU.add)
                    V.scalar_tensor_tensor(out=NS[:, n:n + 1], in0=NS[:, n - 1:n], scalar=dec,
                                           in1=sd[:, 3, 8 + n:9 + n], op0=ALU.mult,
                                           op1=ALU.add).then_inc(*o.up(st_ready if n == 2 else None))

            def mem3(layer, h):
                dve.wait_ge(m3_ps.sem, m3_ps.val(layer, h + 1))
                dve.wait_ge(numl_ready.sem, numl_ready.val(layer, h + 1))
                V.tensor_copy(dn[:, 0:4], sd[:, 3, 0:4])
                V.tensor_copy(dn[:, 5:8], sd[:, 3, 5:8]).then_inc(*o.up())
                for n in (1, 2, 3):
                    w = cols[:, 1, 4 * n + h:4 * n + h + 1]
                    V.scalar_tensor_tensor(out=numh[:, n, :], in0=sd[:, 0, P * n:P * n + P], scalar=w,
                                           in1=numh[:, n, :], op0=ALU.mult, op1=ALU.add).then_inc(*o.up())
                o.settle()
                V.tensor_tensor(dn[:, 5:8], dn[:, 5:8], of_head(1, h)[:, 1:4], ALU.mult).then_inc(*o.up())
                o.settle()
                V.tensor_tensor(dens[:, 1:4], dn[:, 5:8], dn[:, 1:4], ALU.add)
                V.tensor_copy(dens[:, 0:1], dn[:, 0:1]).then_inc(*o.up())
                o.settle()
                V.scalar_tensor_tensor(out=nden[:, :], in0=dens[:, :], scalar=-1.0, in1=dens[:, :],
                                       op0=ALU.mult, op1=ALU.max).then_inc(*o.up())
                o.settle()
                V.tensor_tensor(nden[:, :], nden[:, :], of_head(2, h), ALU.max).then_inc(*o.up())
                o.settle()
                V.reciprocal(dens[:, :], nden[:, :]).then_inc(*o.up())
                o.settle()
                V.tensor_tensor(numh[:, :, :], numh[:, :, :], dens[:, :].unsqueeze(2).broadcast_to([P, NB, P]),
                                ALU.mult).then_inc(*o.up())
                o.settle()
                for n in range(NB):
                    V.bn_stats(bst[:, n, :], numh[:, n, :]).then_inc(*o.up())
                o.settle()
                apart(dve)
                for n in range(NB):
                    V.bn_aggr(bag[:, n, :], bst[:, n, :]).then_inc(*o.up())
                o.settle()
                V.tensor_scalar(rst[:, :], bag[:, :, 1], EPS, None, ALU.add).then_inc(*o.up(mvar))
                dve.wait_ge(mstd.sem, mstd.val(layer, h + 1))
                V.reciprocal(dens[:, :], rst[:, :]).then_inc(*o.up())
                o.settle()
                for n in range(NB):
                    ins = V.tensor_scalar(numh[:, n, :], numh[:, n, :], bag[:, n, 0:1], dens[:, n:n + 1],
                                          ALU.subtract, ALU.mult)
                ins.then_inc(*o.up(hn_ready))

            def mem4(layer, h):
                dve.wait_ge(m4_ps.sem, m4_ps.val(layer, h + 1))
                V.scalar_tensor_tensor(out=ytmp[:, :], in0=sd[:, 0, :], scalar=par[:, PAR_NW + h:PAR_NW + h + 1],
                                       in1=og[:, h, :], op0=ALU.mult, op1=ALU.mult).then_inc(*o.up(ym_ready))
                dve.wait_ge(ym_hi.sem, ym_hi.val(layer, h + 1))
                V.tensor_tensor(yMl[:, h, :], ytmp[:, :], f32(yMh[:, h, :]), ALU.subtract).then_inc(*o.up(ym_lo))

            def conv(layer, c):
                w = [par[:, PAR_CONV + 4 * k + c:PAR_CONV + 4 * k + c + 1] for k in range(3)]
                u, y = cx[:, c, :], convtmp[:, :]
                V.tensor_scalar(y, u, w[2], None, ALU.mult).then_inc(*o.up())
                for k in (1, 0):
                    o.settle()
                    d = 2 - k
                    V.scalar_tensor_tensor(out=y[:, d:], in0=u[:, :SEQ - d], scalar=w[k], in1=y[:, d:],
                                           op0=ALU.mult, op1=ALU.add).then_inc(*o.up())
                o.settle()
                V.tensor_tensor(y, y, cb[:, c, :], ALU.mult).then_inc(*o.up(yc_f))
                dve.wait_ge(yc_hi.sem, yc_hi.val(layer, c + 1))
                V.tensor_tensor(yCl[:, c, :], y, f32(yCh[:, c, :]), ALU.subtract).then_inc(*o.up(yc_lo))
                o.settle()

            def branch(layer, t):
                for m in range(4):
                    k = 4 * (t % 2) + m
                    if m < 3:
                        dve.wait_ge(br_ps.sem, br_ps.val(layer, 3 * t + m + 1))
                    else:
                        dve.wait_ge(slab_done.sem, slab_done.val(layer, S_FFN + 18 + 3 * t + 3))
                    dve.wait_ge(sig_ready.sem, sig_ready.val(layer, 4 * t + m + 1))
                    dst = x[:, k, :] if t < 2 else mtmp[:, :]
                    V.tensor_tensor(dst, pm[m][:, :], gt[:, m, :], ALU.mult).then_inc(*o.up(prod))
                    if t >= 2:
                        o.settle()
                        V.tensor_tensor(x[:, k, :], x[:, k, :], mtmp[:, :], ALU.add).then_inc(*o.up(merged if t >= 4 else None))
                        o.settle()
                    if t >= 4:
                        dve.wait_ge(mg_hi.sem, mg_hi.val(layer, k + 1))
                        V.tensor_tensor(ml[k // 4][:, k % 4, :], x[:, k, :], f32(mh[k // 4][:, k % 4, :]),
                                        ALU.subtract).then_inc(*o.up(mg_lo))

            def projected(layer, s):
                dve.wait_ge(proj.sem, proj.val(layer, proj_count(s)))

            def mixer(layer):
                for s in range(S_MIX):
                    n = S_FFN + s
                    split(layer, n + 1)
                    h, r = divmod(s - 18, 3)
                    if s in (2, 3, 4, 5):
                        memory_gates(layer, s)
                    if 6 <= s < 14:
                        attn_pT(layer, s - 6)
                    if 18 <= s < 30:
                        (mem1, mem3, mem4)[r](layer, h)
                    if s == 39:
                        for m in range(6):
                            centred(layer, 1, m)
                    if s == 0:
                        memory_gates(layer, s)
                        dve.wait_ge(table_ready.sem, 2)
                    if s == 1:
                        rope(layer, 0, q[:, 0, :], 0)
                        rope(layer, 1, q[:, 1, :], 1)
                    if s == 2:
                        rope(layer, 2, q[:, 2, :], 0)
                        rope(layer, 3, q[:, 3, :], 1)
                    if s == 3:
                        rope(layer, 4, kT[:, :], 0)
                    if s == 4:
                        dve.wait_ge(v_ps.sem, v_ps.val(layer, 1))
                        V.tensor_copy(vtok[:, :, :], n4(sd[:, 1, :])).then_inc(*o.up(v_ready))
                    if 5 <= s < 13:
                        attn_scores(layer, s - 5)
                        attn_norm(layer, s - 5)
                    if s == 13:
                        projected(layer, s)
                        for c in range(4):
                            V.tensor_tensor(cx[:, c, :], cx[:, c, :], cc[:, c, :], ALU.mult).then_inc(*o.up(conv_u))
                        o.settle()
                    if s in (15, 16):
                        projected(layer, s - 1)
                        for c in (2 * (s - 15), 2 * (s - 15) + 1):
                            conv(layer, c)
                    if s == 17:
                        projected(layer, s)
                        row_of(layer, 0)
                    if 18 <= s < 30 and r == 0:
                        mem2(layer, h)
                    if 18 <= s < 27 and r == 2:
                        row_of(layer, h + 1)
                    if 18 <= s < 36 and r == 2:
                        branch(layer, h)
                    if s == 23:
                        for c in range(4):
                            dve.wait_ge(ya_hi.sem, ya_hi.val(layer, c + 1))
                            V.tensor_tensor(yAl[:, c, :], yA[:, c, :], f32(yAh[:, c, :]), ALU.subtract).then_inc(*o.up(ya_lo))
                    if s >= 36:
                        dve.wait_ge(slab_done.sem, slab_done.val(layer, n + 1))
                        for m in range(2):
                            residual(layer, 1, 2 * (s - 36) + m, 2 * (s % 2) + m)
                norm_tail(layer, 1)

            with dve.Fori(0, DEPTH) as layer:
                o.layer = layer
                V.tensor_copy(par[:, :].unsqueeze(1), par_all[:, bass.ds(layer, 1), :]).then_inc(*o.up(par_ready))
                o.settle()
                V.tensor_scalar(kbias[:, :], par[:, B_MK:B_MK + 4], float(P) ** -0.5, None, ALU.mult).then_inc(*o.up(kb_ready))
                split(layer, 0)
                ffn(layer, 0, 0)
                mixer(layer)
                ffn(layer, S_FFN + S_MIX, 1)
                o.done()

        @block.tensor
        def _(pe):
            T = nc.tensor

            def slab(layer, n, banks, rh, rl, k_first=0, starts=True, stops=True, it=None, per=0,
                     before_k=None, before_m=None, middle=None, m_outer=False):
                kk, cw = slab_shape(n)
                slot = n % 2
                W, L_ = (w[slot][:, 0:kk * cw].rearrange("p (k c) -> p k c", c=cw) for w in (wh, wl))
                kh = half(n, 1)[0] // cw
                ms = range(len(banks))
                order = [(k, m) for m in ms for k in range(kk)] if m_outer else [(k, m) for k in range(kk) for m in ms]
                seen = set()
                for k, m in order:
                    if (k >= kh) not in seen:
                        seen.add(k >= kh)
                        v = w_lo.val(layer, 2 * n + (2 if k >= kh else 1))
                        pe.wait_ge(w_lo.sem, v if it is None else v + it * 2 * per)
                        if k >= kh and middle is not None:
                            middle()
                    if before_m is not None and k == 0:
                        before_m(m)
                    if before_k is not None and (k, "k") not in seen:
                        seen.add((k, "k"))
                        before_k(k_first + k)
                    hi, lo = W[:, k, P * m:P * m + P], L_[:, k, P * m:P * m + P]
                    out = pm[banks[m]][:, :]
                    a, b = rh(k_first + k), rl(k_first + k)
                    T.matmul(out, hi, a, start=starts and k == 0, stop=False)
                    T.matmul(out, hi, b, start=False, stop=False)
                    ins = T.matmul(out, lo, a, start=False, stop=stops and k == kk - 1)
                    if m_outer and k == kk - 1 and m < len(banks) - 1:
                        ins.then_inc(br_ps.sem, 1)
                ins.then_inc(slab_done.sem, 1)

            def xhk(k):
                return xh[:, k, :]

            def xlk(k):
                return xl[:, k, :]

            def stream_wait(layer, c):
                def wait(k):
                    pe.wait_ge(x_ready.sem, x_ready.val(layer, KD * (c - 1) + k + 1))
                return wait

            def centre_sum(layer, j):
                pe.wait_ge(sum6.sem, sum6.val(layer, j + 1))
                T.matmul(sd[:, 0, :], ones, ln_S[:, :], start=True, stop=True).then_inc(centre_ps.sem, 1)

            def stat_sums(layer, j):
                pe.wait_ge(part_sums.sem, part_sums.val(layer, 5 * j + 5))
                T.matmul(sd[:, 0, :], ones, ln_S[:, :], start=True, stop=False)
                T.matmul(sd[:, 1, :], ones, ln_Q[:, :], start=True, stop=False)
                for m in (6, 7):
                    pe.wait_ge(d_ready.sem, d_ready.val(layer, KD * j + m + 1))
                    ins = T.matmul(sd[:, 0, :], ones, x[:, m, :], start=False, stop=m == 7)
                ins.then_inc(stat_ps.sem, 1)
                for m, t in ((6, ln_s6), (7, ln_s7)):
                    pe.wait_ge(sq_ready.sem, sq_ready.val(layer, KD * j + m + 1))
                    ins = T.matmul(sd[:, 1, :], ones, t[:, :], start=False, stop=m == 7)
                ins.then_inc(stat_ps.sem, 1)

            def ffn(layer, n0, f):
                with pe.Fori(0, 11) as i:
                    pe.wait_ge(silu_ready.sem, silu_ready.val(layer, 22 * f) + i * 2)
                    slab(layer, n0, (0, 1), xhk, xlk, it=i, per=2, before_k=stream_wait(layer, 2 * f))
                    pe.wait_ge(hid_f.sem, hid_f.val(layer, 22 * f) + i * 2)
                    slab(layer, n0 + 1, (2, 3), xhk, xlk, it=i, per=2)

                def hidden(k):
                    pe.wait_ge(hid_l.sem, hid_l.val(layer, 22 * f + k + 1))

                for p in range(4):
                    if p == 0:
                        pe.wait_ge(silu_ready.sem, silu_ready.val(layer, 22 * f + 22))
                    elif p == 1:
                        pe.wait_ge(hid_f.sem, hid_f.val(layer, 22 * f + 22))
                    else:
                        pe.wait_ge(z_ready.sem, z_ready.val(layer, 2 * f * KD + 2 * (p - 1)))
                    for t in range(3):
                        slab(layer, n0 + KF + 3 * p + t, (2 * (p % 2), 2 * (p % 2) + 1),
                             lambda k: hh[:, k, :], lambda k: hl[:, k, :], k_first=8 * t, starts=t == 0, stops=t == 2,
                             before_k=hidden if p == 0 else None,
                             middle=(lambda: centre_sum(layer, 2 * f)) if p == 3 and t == 0 else None)
                stat_sums(layer, 2 * f)

            def gate_products(layer):
                pe.wait_ge(wif_in.sem, wif_in.val(layer, 16))
                pe.wait_ge(x_ready.sem, x_ready.val(layer, KD))
                for n in range(NB):
                    for k in range(KD):
                        ins = T.matmul(sd[:, 3, 8 * n:8 * n + 8], x[:, k, P * n:P * n + P], wif[:, k, :],
                                       start=k == 0, stop=k == KD - 1)
                ins.then_inc(gate_ps.sem, 1)

            def rotate(layer, r, t, bank, s):
                pe.wait_ge(proj.sem, proj.val(layer, proj_count(s)))
                if r >= 2:
                    pe.wait_ge(rot_used.sem, rot_used.val(layer, r - 1))
                T.matmul(sd[:, bank, :], const[:, K_ROT:K_ROT + P], t, start=True, stop=True).then_inc(rot_ps.sem, 1)

            def middle_job(layer, s):
                if s == 0:
                    gate_products(layer)
                if s == 2:
                    pe.wait_ge(gates_tok.sem, gates_tok.val(layer, 1))
                    T.transpose(sd[0:16, 2, 0:128], gf[:, :], ident)
                    T.transpose(sd[0:16, 2, 128:256], gi[:, :], ident).then_inc(rows_ps.sem, 1)
                if s == 3:
                    pe.wait_ge(scans.sem, scans.val(layer, 1))
                    apart(pe)
                    T.transpose(sd[0:1, 2, 256:272], rb[:, 127:128], ident[0:16, 0:16])
                    T.transpose(sd[0:1, 2, 272:288], rloc[:, 127:128], ident[0:16, 0:16]).then_inc(ends_ps.sem, 1)
                if s == 4:
                    pe.wait_ge(carry.sem, carry.val(layer, 1))
                    apart(pe)
                    T.transpose(sd[0:16, 2, 300:301], mrow[0:1, 32:48], ident[0:1, 0:1])
                    T.transpose(sd[0:16, 2, 301:302], mrow[0:1, 48:64], ident[0:1, 0:1]).then_inc(carry_ps.sem, 1)
                if s == 5:
                    pe.wait_ge(exp_rows.sem, exp_rows.val(layer, 1))
                    apart(pe)
                    for i, row in enumerate((ra, rf, ri, rb)):
                        T.transpose(sd[:, 3, 16 * i:16 * i + 16], row[:, :], ident[0:16, 0:16])
                    T.matmul(sd[:, 3, 64:80], ones[0:1, :], mrow[0:1, 80:96], start=True, stop=True).then_inc(cols_ps.sem, 1)
                if 6 <= s < 14:
                    u = s - 6
                    b = sx[u % 2]
                    pe.wait_ge(p_ready.sem, p_ready.val(layer, u + 1))
                    if u == 0:
                        pe.wait_ge(cols_ready.sem, cols_ready.val(layer, 1))
                    else:
                        pe.wait_ge(o_used.sem, o_used.val(layer, u))
                    for w in ((0, 1) if u >= 2 else (1,)):
                        for j in range(4):
                            ins = T.transpose(sd[:, 2 + w, P * j:P * j + P], b[:, j, P * w:P * w + P], ident)
                    ins.then_inc(pT_ps.sem, 1)
                if 18 <= s < 30:
                    h, r = divmod(s - 18, 3)
                    if r == 0:
                        if h == 0:
                            pe.wait_ge(o_used.sem, o_used.val(layer, 8))
                            pe.wait_ge(pT_dve.sem, pT_dve.val(layer, 8))
                            pe.wait_ge(proj.sem, proj.val(layer, proj_count(9)))
                        else:
                            pe.wait_ge(ym_ready.sem, ym_ready.val(layer, h))
                        pe.wait_ge(rowx_ready.sem, rowx_ready.val(layer, h + 1))
                        T.matmul(sd[:, 1, :], ones[0:16, :], rowx[:, :, :].rearrange("p n t -> p (n t)"), start=True, stop=True)
                        for n in range(NB):
                            c = slice(P * n, P * n + P)
                            T.matmul(sd[:, 0, c], mk[:, h, c], mq[:, h, c], start=True, stop=True)
                        for n in range(NB):
                            c = slice(P * n, P * n + P)
                            T.transpose(sd[:, 2, c], mk[:, h, c], ident)
                        for n in range(NB):
                            c = slice(P * n, P * n + P)
                            ins = T.transpose(sd[:, 3, c], mv[:, h, c], ident)
                        ins.then_inc(m1_ps.sem, 1)
                    if r == 1:
                        pe.wait_ge(st_ready.sem, st_ready.val(layer, h + 1))
                        for n in (1, 2, 3):
                            c = slice(P * n, P * n + P)
                            T.matmul(sd[:, 0, c], mq[:, h, c], CS[:, n - 1, :], start=True, stop=True)
                            ins = T.matmul(sd[:, 3, 4 + n:5 + n], mq[:, h, c], NS[:, n - 1:n], start=True, stop=True)
                        ins.then_inc(m3_ps.sem, 1)
                    if r == 2:
                        pe.wait_ge(hn_ready.sem, hn_ready.val(layer, h + 1))
                        for n in range(NB):
                            ins = T.transpose(sd[:, 0, P * n:P * n + P], numh[:, n, :], ident)
                        ins.then_inc(m4_ps.sem, 1)
                if s == 39:
                    centre_sum(layer, 1)

            def end_job(layer, s):
                if s == 1:
                    rotate(layer, 0, q[:, 0, :], 0, 0)
                    rotate(layer, 1, q[:, 1, :], 1, 0)
                if s == 2:
                    rotate(layer, 2, q[:, 2, :], 0, 1)
                    rotate(layer, 3, q[:, 3, :], 1, 1)
                if s == 3:
                    rotate(layer, 4, kT[:, :], 0, 2)
                if s == 4:
                    pe.wait_ge(proj.sem, proj.val(layer, proj_count(3)))
                    pe.wait_ge(rot_used.sem, rot_used.val(layer, 4))
                    for n in range(NB):
                        ins = T.transpose(sd[:, 1, P * n:P * n + P], vT[:, P * n:P * n + P], ident)
                    ins.then_inc(v_ps.sem, 1)
                if 6 <= s < 14:
                    u = s - 6
                    blk, g = divmod(u, 2)
                    pe.wait_ge(pT_dve.sem, pT_dve.val(layer, u + 1))
                    if u >= 2:
                        pe.wait_ge(pT_act.sem, pT_act.val(layer, u - 1))
                    ws = (0, 1) if u >= 2 else (1,)
                    for par_ in range(2):
                        for w in ws:
                            rhs = pT[:, w, :].rearrange("p (a b t) -> p a b t", a=2, b=2)[:, :, par_, :]
                            ins = T.matmul(sd[HD * par_:HD * par_ + HD, 2, 0:256].rearrange("p (a t) -> p a t", a=2),
                                           vtok[:, blk - 1 + w, HD * g:HD * g + HD], rhs, start=w == ws[0], stop=w == 1)
                    ins.then_inc(o_ps.sem, 1)
                if 5 <= s < 13:
                    u = s - 5
                    blk, g = divmod(u, 2)
                    if u == 0:
                        pe.wait_ge(roped.sem, roped.val(layer, 5))
                        pe.wait_ge(v_ready.sem, v_ready.val(layer, 1))
                    else:
                        pe.wait_ge(sc_max.sem, sc_max.val(layer, u))
                    half_ = slice(HD * g, HD * g + HD)
                    k0 = 1 if u < 2 else 0
                    for j in range(4):
                        ins = T.matmul(sd[:, j // 2, 256 * (j % 2) + P * k0:256 * (j % 2) + 256],
                                       q[half_, j, P * blk:P * blk + P], kT[half_, P * (blk - 1 + k0):P * (blk + 1)],
                                       start=True, stop=True)
                    ins.then_inc(sc_ps.sem, 1)
                if 18 <= s < 30 and (s - 18) % 3 == 0:
                    h = (s - 18) // 3
                    pe.wait_ge(s_ready.sem, s_ready.val(layer, h + 1))
                    pe.wait_ge(vt_ready.sem, vt_ready.val(layer, h + 1))
                    for n in range(NB):
                        T.matmul(sd[:, 1, P * n:P * n + P], Dm[:, n, :], vt[:, n, :], start=True, stop=True)
                        T.matmul(sd[:, 3, n:n + 1], Dm[:, n, :], ones[:, 0:1], start=True, stop=True)
                    for n in range(NB - 1):
                        T.matmul(sd[:, 2, P * n:P * n + P], kw[:, n, :], vt[:, n, :], start=True, stop=True)
                        ins = T.matmul(sd[:, 3, 8 + n:9 + n], kw[:, n, :], ones[:, 0:1], start=True, stop=True)
                    ins.then_inc(m2_ps.sem, 1)

            def mixer(layer):
                for s in range(S_MIX):
                    n = S_FFN + s
                    t, r = divmod(s - 18, 3)
                    mid = lambda: middle_job(layer, s)
                    pair = (2 * (s % 2), 2 * (s % 2) + 1)
                    if 2 <= s < 18:
                        pe.wait_ge(proj.sem, proj.val(layer, proj_count(s - 2)))
                    if s < 2:
                        slab(layer, n, pair, xhk, xlk, middle=mid,
                             before_k=stream_wait(layer, 1) if s == 0 else None)
                    elif s < 4:
                        slab(layer, n, pair[0:1], xhk, xlk, middle=mid)
                    elif s < 18:
                        slab(layer, n, pair, xhk, xlk, middle=mid)
                    elif s < 36 and r < 2:
                        if t == 0:
                            pe.wait_ge(proj.sem, proj.val(layer, proj_count(16 + r)))
                        else:
                            pe.wait_ge(prod.sem, prod.val(layer, 4 * (t - 1) + 2 * r + 2))
                        slab(layer, n, (2 * r, 2 * r + 1), xhk, xlk, middle=mid)
                    elif s < 36:
                        bh, bl, ready = ((yCh, yCl, yc_lo), (yAh, yAl, ya_lo), (yMh, yMl, ym_lo))[t // 2]
                        pe.wait_ge(ready.sem, ready.val(layer, 4))
                        middle_job(layer, s)
                        slab(layer, n, (0, 1, 2, 3), lambda k: bh[:, k, :], lambda k: bl[:, k, :], m_outer=True,
                             before_m=lambda m: pe.wait_ge(sig_ready.sem, sig_ready.val(layer, 4 * t + m + 1)))
                    else:
                        if s < 38:
                            pe.wait_ge(prod.sem, prod.val(layer, 20 + 2 * (s - 36) + 2))
                        else:
                            pe.wait_ge(z_ready.sem, z_ready.val(layer, KD + 2 * (s - 37)))
                        slab(layer, n, pair, lambda k: mh[k // 4][:, k % 4, :], lambda k: ml[k // 4][:, k % 4, :], middle=mid,
                             before_k=(lambda k: pe.wait_ge(mg_lo.sem, mg_lo.val(layer, k + 1))) if s == 36 else None)
                    end_job(layer, s)
                stat_sums(layer, 1)

            pe.sem_inc(slab_done.sem, 1)
            pe.sem_inc(gate_ps.sem, 1)
            with pe.Fori(0, DEPTH) as layer:
                ffn(layer, 0, 0)
                mixer(layer)
                ffn(layer, S_FFN + S_MIX, 1)


def proj_count(s):
    return 2 * (s + 1) if s < 2 else s + 3 if s < 4 else 6 + 2 * (s - 3)


SETUP_STEPS = 11


def params(b_in, attn_sinks, mlstm_norm_w, conv_w, ln_w, ln_b):
    out = np.zeros((DEPTH, P, NPAR), np.float32)
    for la in range(DEPTH):
        b = b_in[la]
        bq = b[C_AQ:C_AQ + 512].reshape(2, 4, HD)
        for j in range(4):
            out[la, :, B_Q + j] = np.concatenate([bq[0, j], bq[1, j]])
        for col, c, n in ((B_K, C_AK, 1), (B_V, C_AV, 1), (B_MQ, C_MQ, 16), (B_CX, C_CX, 4),
                          (B_CC, C_CX + 2 * WB, 4), (B_CB, C_CX + WB, 4), (B_G, C_GATE, 24)):
            out[la, :, col:col + n] = b[c:c + P * n].reshape(n, P).T
        for j in range(3):
            for w, t in enumerate((ln_w, ln_b)):
                c = PAR_LN + 16 * j + 8 * w
                out[la, :, c:c + 8] = t[la, j].reshape(KD, P).T
        out[la, :, PAR_NW:PAR_NW + 4] = mlstm_norm_w[la].reshape(MH, P).T
        for k in range(3):
            out[la, :, PAR_CONV + 4 * k:PAR_CONV + 4 * k + 4] = conv_w[la, k].reshape(4, P).T
        out[la, :, PAR_IF:PAR_IF + 8] = b[C_IF:C_IF + 8]
        out[la, :, PAR_SINK:PAR_SINK + 8] = attn_sinks[la]
    return out


def constants():
    c = np.zeros((P, NCONST), np.float32)
    i, j = np.arange(P)[:, None], np.arange(P)[None, :]
    c[:, K_ID:K_ID + P] = i == j
    c[:, K_ONE:K_ONE + P] = 1.0
    half = ROT // 2
    for h in (0, HD):
        for d in range(half):
            c[h + d + half, K_ROT + h + d] = -1.0
            c[h + d, K_ROT + h + d + half] = 1.0
            c[h + d, K_FREQ] = c[h + d + half, K_FREQ] = THETA ** (-2.0 * d / ROT)
    c[:, K_MASK:K_MASK + P] = np.where(j > i, 0.0, NEG)
    c[:, K_MASK + P:K_MASK + 2 * P] = np.where(j <= i, 0.0, NEG)
    c[:, K_MT:K_MT + P] = np.where(j >= i, 0.0, NEG)
    for h in range(MH):
        for n in range(NB):
            c[4 * n + h, K_HM + 4 * h + n] = 1.0
    return c


def kernel(x, positions, w_in, b_in, attn_sinks, mlstm_norm_w, conv_w, w_branch, w_out,
           ffn1_w_gu, ffn1_w_down, ffn2_w_gu, ffn2_w_down, ln_w, ln_b):
    import concourse.bacc as bacc
    from concourse.bass_utils import run_bass_kernel_spmd

    a = {k: np.asarray(v) for k, v in dict(
        b_in=b_in, attn_sinks=attn_sinks, mlstm_norm_w=mlstm_norm_w, conv_w=conv_w, ln_w=ln_w, ln_b=ln_b).items()}
    arrays = {
        "xT": np.ascontiguousarray(np.asarray(x)[0].T), "positions": np.asarray(positions),
        "w_in": np.asarray(w_in), "w_branch": np.asarray(w_branch), "w_out": np.asarray(w_out),
        "gu1": np.asarray(ffn1_w_gu), "down1": np.asarray(ffn1_w_down),
        "gu2": np.asarray(ffn2_w_gu), "down2": np.asarray(ffn2_w_down),
        "par": params(**a), "constants": constants(),
    }
    nc = bacc.Bacc("TRN2", target_bir_lowering=False, num_devices=1)
    args = [nc.dram_tensor(n, v.shape, mybir.dt.from_np(v.dtype), kind="ExternalInput").ap() for n, v in arrays.items()]
    outT = nc.dram_tensor("outT", (D, SEQ), F32, kind="ExternalOutput").ap()
    build(nc, *args, outT)
    r = run_bass_kernel_spmd(nc, [arrays], core_ids=[0])
    return np.ascontiguousarray(r.results[0]["outT"].T)[None]
```

```python
from contextlib import ExitStack

import concourse.bass as bass
import numpy as np
from concourse import mybir

F32 = mybir.dt.float32
F32R = mybir.dt.float32r
I32 = mybir.dt.int32
ALU = mybir.AluOpType
ACT = mybir.ActivationFunctionType
AX = mybir.AxisListType

P = 128
SEQ, D, DEPTH = 512, 1024, 2
KD = D // P
DFF = 2816
KF = DFF // P
NB = SEQ // P
HD = 64
NQ, NKV = 8, 2
MH = 4
ROT = HD // 4
THETA = 500000.0
WB = 512
KB = WB // P
EPS = 1e-5
ALPHA = (2.0 * DEPTH) ** 0.25
NEG = -1e30
P_IN = 7432
TWO_PI = 2.0 * np.pi

C_AQ, C_AK, C_AV, C_MQ = 0, 512, 640, 768
C_MO, C_IF, C_CX = 2304, 2816, 2824
C_GATE = C_CX + 3 * WB
B_Q, B_K, B_V, B_MQ, B_MK, B_MV, B_MO, B_CX, B_CC, B_CB, B_G = 0, 4, 5, 6, 10, 14, 18, 22, 26, 30, 34
PAR_LN = 58
PAR_NW = PAR_LN + 48
PAR_CONV = PAR_NW + 4
PAR_IF = PAR_CONV + 12
PAR_SINK = PAR_IF + 8
NPAR = PAR_SINK + 8
K_ID, K_ONE, K_ROT, K_MASK, K_MT, K_FREQ = 0, 128, 256, 384, 640, 768
K_HM = 769
NCONST = K_HM + 16

S_FFN = KF + 12
S_MIX = 40
S_LAYER = 2 * S_FFN + S_MIX
OWN = {"scalar": 3, "vector": 206, "gpsimd": 15}
CENTRE = 2
POOLED = 6
BRANCH_ORDER = (2, 0, 1)


def build(nc, xT, positions, w_in, w_branch, w_out, gu1, down1, gu2, down2, par_in, const_in, outT):
    ctx = ExitStack()
    with ctx:
        base = (nc.sbuf_base + 127) // 128 * 128
        top = [base]

        def at(name, shape, dt, offset):
            return nc.alloc_sbuf_tensor_at(name, shape, dt, offset=offset)

        def place(name, shape, dt=F32):
            size = int(np.prod(shape[1:])) * 4
            t = at(name, shape, dt, top[0])
            top[0] += (size + 31) // 32 * 32
            return t

        KB1 = 1024
        x_at = top[0]
        x = place("x", [P, KD, SEQ])
        xh = place("xh", [P, KD, SEQ], F32R)
        xl = place("xl", [P, KD, SEQ], F32R)
        raw = [place(f"raw{i}", [P, 2048]) for i in range(2)]
        wh = [place(f"wh{i}", [P, 2048], F32R) for i in range(2)]
        wl = [place(f"wl{i}", [P, 2048], F32R) for i in range(2)]
        big_at = top[0]
        hh = place("hh", [P, KF, SEQ], F32R)
        hl = place("hl", [P, KF, SEQ], F32R)

        def big(name, kb, shape, dt=F32):
            return at(name, shape, dt, big_at + int(kb * KB1))

        q = big("q", 0, [P, 4, SEQ])
        kT = big("kT", 8, [P, SEQ])
        vtok = big("vtok", 10, [P, NB, P])
        mq = big("mq", 12, [P, MH, SEQ])
        mk = big("mk", 20, [P, MH, SEQ])
        mv = big("mv", 28, [P, MH, SEQ])
        cx = big("cx", 36, [P, 4, SEQ])
        cc = big("cc", 44, [P, 4, SEQ])
        cb = big("cb", 52, [P, 4, SEQ])
        gt = big("gt", 68, [P, 4, SEQ])
        yA = big("yA", 76, [P, 4, SEQ])
        vT = big("vT", 84, [P, SEQ])
        mtmp = big("mtmp", 84, [P, SEQ])
        ropetmp = big("ropetmp", 86, [P, SEQ])
        convtmp = big("convtmp", 86, [P, SEQ])
        og = big("og", 44, [P, 4, SEQ])
        yCl = big("yCl", 0, [P, 4, SEQ], F32R)
        yCh = big("yCh", 60, [P, 4, SEQ], F32R)
        yAl = big("yAl", 0, [P, 4, SEQ], F32R)
        yAh = big("yAh", 60, [P, 4, SEQ], F32R)
        yMh = big("yMh", 36, [P, 4, SEQ], F32R)
        yMl = big("yMl", 52, [P, 4, SEQ], F32R)
        mh = [big(f"mh{i}", (12, 20)[i], [P, 4, SEQ], F32R) for i in range(2)]
        ml = [big(f"ml{i}", (28, 60)[i], [P, 4, SEQ], F32R) for i in range(2)]
        CS = big("CS", 8, [P, 3, P])
        ytmp = big("ytmp", 10, [P, SEQ])
        ln_M = big("ln_M", 68, [P, SEQ])
        sx = [at(f"sx{i}", [P, 4, 256], F32, x_at + 4 * KB1 * i) for i in range(2)]
        pT = at("pT", [P, 2, SEQ], F32, x_at + 8 * KB1)

        const = place("const", [P, NCONST])
        cosT = place("cosT", [P, SEQ])
        sinT = place("sinT", [P, SEQ])
        par_all = place("par_all", [P, DEPTH, NPAR])
        par = place("par", [P, NPAR])
        kbias = place("kbias", [P, MH])
        NS = place("NS", [P, 3])
        cols = place("cols", [P, 5, 16])
        gi = place("gi", [P, 16])
        gf = place("gf", [P, 16])
        gs = place("gs", [P, 16])
        mx = place("mx", [P, 4])
        nmx = place("nmx", [P, 4])
        es = place("es", [P, 4])
        sums = place("sums", [P, 4])
        dn = place("dn", [P, 12])
        dens = place("dens", [P, 4])
        nden = place("nden", [P, 4])
        bst = place("bst", [P, 4, 6])
        bag = place("bag", [P, 4, 2])
        rst = place("rst", [P, 4])
        mrow = place("mrow", [1, 96])
        wif = place("wif", [P, KD, 8])
        lut = place("lut", [P, 1])
        tok = place("tok", [P, 5, NB])
        t_at = top[0]

        def tmp(name, kb, shape, dt=F32):
            assert t_at + int(kb * KB1) + int(np.prod(shape[1:])) * 4 <= nc.sbuf_usable_end
            return at(name, shape, dt, t_at + int(kb * KB1))

        ln_S = tmp("ln_S", 0, [P, SEQ])
        ln_Q = tmp("ln_Q", 2, [P, SEQ])
        ln_C = tmp("ln_C", 4, [P, SEQ])
        ln_sq = [tmp(f"ln_sq{i}", 6 + 2 * i, [P, SEQ]) for i in range(2)]
        sil = [tmp(f"sil{i}", 2 * i, [P, SEQ]) for i in range(2)]
        hp = [tmp(f"hp{i}", 4 + 2 * i, [P, SEQ]) for i in range(2)]
        rf, ri, rb, ra, rloc, rg, rm, rz = (tmp(f"row{i}", 0.5 * i, [16, P]) for i in range(8))
        rowx = tmp("rowx", 4, [16, NB, P])
        Dm = tmp("Dm", 6, [P, NB, P])
        kw = tmp("kw", 8, [P, NB, P])
        vt = tmp("vt", 10, [P, NB, P])
        numh = big("numh", 86, [P, NB, P])
        ident = const[:, K_ID:K_ID + P]
        ones = const[:, K_ONE:K_ONE + P]

        pm = [ctx.enter_context(nc.psum_tensor(f"main{i}", [P, SEQ], F32)) for i in range(4)]
        sd = ctx.enter_context(nc.psum_tensor("side", [P, 4, SEQ], F32))

        class Signal:

            def __init__(self, name, per_layer, start=0, lead=0):
                self.sem, self.lead = ctx.enter_context(nc.semaphore(name)), lead
                self.name, self.per, self.start = name, per_layer, start

            def val(self, layer, count):
                assert count + self.start > 0, self.name
                return layer * self.per + (count + self.start)

        class Order:

            def __init__(self, eng, own):
                self.eng, self.own = eng, own
                self.n, self.last, self.loop, self.layer = {}, None, None, 0

            def up(self, sig=None):
                sig = sig or self.own
                self.n[sig] = self.n.get(sig, 0) + 1
                self.last = sig
                return sig.sem, 1

            def settle(self):
                sig = self.last
                v = sig.val(self.layer, self.n[sig])
                if self.loop is not None:
                    i, per = self.loop
                    v = v + i * per[sig]
                self.eng.wait_ge(sig.sem, v)

            def enter(self, i, per):
                self.loop, self.was = (i, per), dict(self.n)

            def leave(self, times):
                i, per = self.loop
                for sig in self.n:
                    d = self.n[sig] - self.was.get(sig, 0)
                    assert d == per.get(sig, 0), (d, per.get(sig, 0))
                    self.n[sig] += d * (times - 1)
                self.loop = None

            def done(self):
                for sig, n in self.n.items():
                    assert n == sig.per + sig.lead, (sig.name, n, sig.per)

        own_act = Signal("own_act", OWN["scalar"])
        own_dve = Signal("own_dve", OWN["vector"])
        own_pool = Signal("own_pool", OWN["gpsimd"])
        raw_in = [[Signal(f"raw_in{s}{h}", 16 * (S_LAYER // 2 + 1)) for h in range(2)] for s in range(2)]
        wif_in = Signal("wif_in", 16)
        start_in = Signal("start_in", 0)
        x_in = [Signal(f"x_in{k}", 0) for k in range(4)]
        pos_in = Signal("pos_in", 0)
        out_done = Signal("out_done", 0)
        w_hi = Signal("w_hi", 2 * S_LAYER, lead=2)
        w_lo = Signal("w_lo", 2 * S_LAYER, start=3, lead=2)
        slab_done = Signal("slab_done", S_LAYER, start=1)
        passed = Signal("passed", 0)
        setup = Signal("setup", 0)
        table_ready = Signal("table_ready", 0)
        x_ready = Signal("x_ready", 3 * KD, start=KD)
        xhi_ready = Signal("xhi_ready", 3 * KD, start=KD)
        par_ready = Signal("par_ready", 1)
        silu_ready = Signal("silu_ready", 4 * 11, start=1)
        hid_f = Signal("hid_f", 4 * 11, start=1)
        hid_h = Signal("hid_h", 4 * 11)
        hid_l = Signal("hid_l", 4 * 11)
        z_ready = Signal("z_ready", 3 * CENTRE)
        cen_ready = Signal("cen_ready", 3 * (KD - 1))
        z_sum = Signal("z_sum", 3)
        centre_ps = Signal("centre_ps", 3)
        centre = Signal("centre", 3)
        d_ready = Signal("d_ready", 3 * KD)
        sq_ready = Signal("sq_ready", 3 * KD)
        part_sums = Signal("part_sums", 3 * (POOLED - 1))
        seventh_ps = Signal("seventh_ps", 3)
        sums_ready = Signal("sums_ready", 3)
        stat_ps = Signal("stat_ps", 3 * 2)
        var_ready = Signal("var_ready", 3)
        root_ready = Signal("root_ready", 3)
        diag_ready = Signal("diag_ready", 3 * 2)
        wide_ps = Signal("wide_ps", 3 * 2)
        mean_wide = Signal("mean_wide", 3)
        scaled = Signal("scaled", 3 * KD)
        norm_ready = Signal("norm_ready", 3 * KD, start=1)
        proj = Signal("proj", 34)
        gate_ps = Signal("gate_ps", 1, start=1)
        rot_ps = Signal("rot_ps", 5)
        rot_used = Signal("rot_used", 5)
        roped = Signal("roped", 5)
        kb_ready = Signal("kb_ready", 1)
        v_ps = Signal("v_ps", 1)
        v_ready = Signal("v_ready", 1)
        f_abs = Signal("f_abs", 1)
        f_exp = Signal("f_exp", 1)
        f_one = Signal("f_one", 1)
        f_ln = Signal("f_ln", 1)
        gates_tok = Signal("gates_tok", 1)
        gate_in = Signal("gate_in", 1)
        rows_ps = Signal("rows_ps", 1)
        rows_in = Signal("rows_in", 1)
        scans = Signal("scans", 1)
        ends_ps = Signal("ends_ps", 1)
        carry = Signal("carry", 1)
        carry_ps = Signal("carry_ps", 1)
        g_rows = Signal("g_rows", 1)
        decay_row = Signal("decay_row", 1)
        exp_rows = Signal("exp_rows", 1)
        cols_ps = Signal("cols_ps", 1)
        cols_ready = Signal("cols_ready", 1)
        sc_ps = Signal("sc_ps", 8)
        sc_max = Signal("sc_max", 8)
        sc_exp = Signal("sc_exp", 8)
        p_ready = Signal("p_ready", 8)
        pT_ps = Signal("pT_ps", 8)
        pT_act = Signal("pT_act", 6)
        pT_dve = Signal("pT_dve", 8)
        o_ps = Signal("o_ps", 8)
        o_used = Signal("o_used", 8)
        rowx_ready = Signal("rowx_ready", MH)
        m1_ps = Signal("m1_ps", MH)
        dm_ready = Signal("dm_ready", MH)
        dexp = Signal("dexp", MH)
        vt_ready = Signal("vt_ready", MH)
        s_ready = Signal("s_ready", MH)
        m2_ps = Signal("m2_ps", MH)
        numl_ready = Signal("numl_ready", MH)
        st_ready = Signal("st_ready", MH)
        m3_ps = Signal("m3_ps", MH)
        mvar = Signal("mvar", MH)
        mstd = Signal("mstd", MH)
        hn_ready = Signal("hn_ready", MH)
        m4_ps = Signal("m4_ps", MH)
        ym_ready = Signal("ym_ready", MH)
        ym_hi = Signal("ym_hi", MH)
        ym_lo = Signal("ym_lo", MH)
        conv_u = Signal("conv_u", 4)
        yc_f = Signal("yc_f", 4)
        yc_hi = Signal("yc_hi", 4)
        yc_lo = Signal("yc_lo", 4)
        ya_hi = Signal("ya_hi", 4)
        ya_lo = Signal("ya_lo", 4)
        sig_ready = Signal("sig_ready", 24)
        br_ps = Signal("br_ps", 18)
        prod = Signal("prod", 24)
        merged = Signal("merged", 8)
        mg_hi = Signal("mg_hi", 8)
        mg_lo = Signal("mg_lo", 8)

        def f32(a):
            return a.bitcast(F32)

        def slab_shape(n):
            if n < KF or n == S_LAYER:
                return 8, 256
            if n < S_FFN:
                return (8, 8, 6)[(n - KF) % 3], 256
            if n < S_FFN + S_MIX:
                s = n - S_FFN
                if s in (2, 3):
                    return 8, 128
                if 18 <= s < 36 and (s - 18) % 3 == 2:
                    return 4, 512
                return 8, 256
            return slab_shape(n - S_FFN - S_MIX)

        def half(n, h):
            k, c = slab_shape(n)
            first = k // 2 if k != 6 else 4
            return (0, first * c) if h == 0 else (first * c, k * c)

        def apart(eng):
            eng.sem_inc(passed.sem, 1)

        def pieces(n, h):
            a, b = half(n, h)
            if n not in (S_FFN, S_FFN + 1):
                return [(lambda t: t[:, a:b], lambda t: t[:, a:b])]

            def read(j):
                return lambda t: t[:, a:b].rearrange("p (k b j c) -> p k j b c", b=2, j=2, c=HD)[:, :, j]

            def write(j):
                return lambda t: t[:, a:b].rearrange("p (k j b c) -> p k j b c", j=2, b=2, c=HD)[:, :, j]

            return [(read(j), write(j)) for j in range(2)]

        block = ctx.enter_context(nc.Block())

        @block.sync
        def _(sp):
            def load(layer, n, slot, src, it=None, per=0, count=0):
                v = w_lo.val(layer, 2 * n - 2)
                sp.wait_ge(w_lo.sem, v if it is None else v + it * 2 * per)
                apart(sp)
                kk = src.shape[1]
                k0 = kk // 2 if kk != 6 else 4
                cols_ = int(np.prod(src.shape[2:]))
                for h, (a, b) in enumerate(((0, k0), (k0, kk))):
                    dst = raw[slot][:, a * cols_:b * cols_].rearrange("p (k c) -> p k c", c=cols_)
                    if len(src.shape) == 4:
                        for g in range(2):
                            sp.dma_start(dst[:, :, 128 * g:128 * g + 128], src[:, a:b, g]).then_inc(raw_in[slot][h].sem, 16)
                    else:
                        sp.dma_start(dst, src[:, a:b]).then_inc(raw_in[slot][h].sem, 16)

            def tiles(w, layer):
                return w[layer].rearrange("(k p) n -> p k n", p=P)

            def gate_up(layer, n, gu, j, i, it=None, of=None):
                load(layer, n, j, tiles(gu, layer if of is None else of)[:, :, bass.ds(i * 256 + j * DFF, 256)], it=it, per=2)

            def ffn(layer, n0, gu, down):
                wd = tiles(down, layer)
                with sp.Fori(0, 10) as i:
                    gate_up(layer, n0 + 1, gu, 1, i, it=i)
                    gate_up(layer, n0 + 2, gu, 0, i + 1, it=i)
                gate_up(layer, n0 + 21, gu, 1, 10)
                for p in range(4):
                    for t in range(3):
                        n = n0 + KF + 3 * p + t
                        src = wd[:, 8 * t:min(8 * t + 8, KF), 256 * p:256 * p + 256]
                        load(layer, n, n % 2, src)

            first = tiles(gu1, 0)
            for h in range(2):
                sp.dma_start(raw[0][:, 1024 * h:1024 * h + 1024].rearrange("p (k c) -> p k c", c=256),
                             first[:, 4 * h:4 * h + 4, 0:256]).then_inc(raw_in[0][h].sem, 16)
                for k in (2 * h, 2 * h + 1):
                    sp.dma_start(x[:, 2 * k:2 * k + 2, :],
                                 xT.rearrange("(k p) t -> p k t", p=P)[:, 2 * k:2 * k + 2]).then_inc(x_in[k].sem, 16)

            tables = ((const[:, :], const_in, start_in), (par_all[:, :, :], par_in.rearrange("l p n -> p l n"), start_in),
                      (mq[:, 0, :].bitcast(I32), positions[0, :].partition_broadcast(P), pos_in))
            for dst, src, sig in tables:
                sp.dma_start(dst, src).then_inc(sig.sem, 16)
            with sp.Fori(0, DEPTH) as layer:
                ffn(layer, 0, gu1, down1)
                wi, wo = tiles(w_in, layer), tiles(w_out, layer)
                sp.wait_ge(gate_ps.sem, gate_ps.val(layer, 0))
                apart(sp)
                sp.dma_start(wif[:, :, :], wi[:, :, C_IF:C_IF + 8]).then_inc(wif_in.sem, 16)
                for s in range(S_MIX):
                    n = S_FFN + s
                    if s < 2:
                        src = wi[:, :, 0:512].rearrange("p k (b c) -> p k b c", b=2)[:, :, :, 128 * s:128 * s + 128]
                    elif s < 4:
                        src = wi[:, :, C_AK + 128 * (s - 2):C_AK + 128 * (s - 1)]
                    elif s < 10:
                        src = wi[:, :, C_MQ + 256 * (s - 4):C_MQ + 256 * (s - 3)]
                    elif s < 18:
                        c = {0: C_CX, 1: C_CX + 2 * WB, 2: C_CX + WB, 3: C_MO}[(s - 10) // 2] + 256 * (s % 2)
                        src = wi[:, :, c:c + 256]
                    elif s < 36:
                        t, r = divmod(s - 18, 3)
                        br, quad = BRANCH_ORDER[t // 2], t % 2
                        if r < 2:
                            c = C_GATE + br * D + quad * 512 + r * 256
                            src = wi[:, :, c:c + 256]
                        else:
                            src = w_branch[layer][br].rearrange("(k p) n -> p k n", p=P)[:, :, quad * 512:quad * 512 + 512]
                    else:
                        src = wo[:, :, 256 * (s - 36):256 * (s - 35)]
                    load(layer, n, n % 2, src)
                n = S_FFN + S_MIX
                gate_up(layer, n, gu2, 0, 0)
                ffn(layer, n, gu2, down2)
                gate_up(layer, S_LAYER, gu1, 0, 0, of=DEPTH - 1)
            for k in range(KD):
                sp.wait_ge(norm_ready.sem, norm_ready.val(DEPTH - 1, 2 * KD + k + 1))
                sp.dma_start(outT[P * k:P * (k + 1), :], x[:, k, :]).then_inc(out_done.sem, 16)
            sp.wait_ge(out_done.sem, 16 * KD)

        @block.scalar
        def _(act):
            o = Order(act, own_act)
            act.sem_inc(silu_ready.sem, 1)
            act.sem_inc(norm_ready.sem, 1)

            def split(layer, n, it=None, per=0):
                v = slab_done.val(layer, n - 1)
                act.wait_ge(slab_done.sem, v if it is None else v + it * per)
                for h in range(2):
                    split_half(layer, n, h, it, per)

            def split_half(layer, n, h, it=None, per=0):
                slot = n % 2
                v = raw_in[slot][h].val(layer, 16 * (n // 2 + 1 + (n >= S_FFN)))
                act.wait_ge(raw_in[slot][h].sem, v if it is None else v + it * 16 * (per // 2))
                for get, put in pieces(n, h):
                    ins = act.activation(put(wh[slot]), get(raw[slot]), ACT.Copy)
                ins.then_inc(*o.up(w_hi))

            def start():
                for h in range(2):
                    split_half(0, 0, h)
                    for k in range(4 * h, 4 * h + 4):
                        act.wait_ge(x_in[k // 2].sem, 16)
                        act.activation(xh[:, k, :], x[:, k, :], ACT.Copy).then_inc(xhi_ready.sem, 1)
                act.wait_ge(setup.sem, SETUP_STEPS)
                act.activation(sinT[:, :], mq[:, 0, :], ACT.Sin).then_inc(table_ready.sem, 1)
                act.activation(cosT[:, :], mq[:, 1, :], ACT.Sin).then_inc(table_ready.sem, 1)

            def centre_copy(layer, j):
                act.wait_ge(centre_ps.sem, centre_ps.val(layer, j + 1))
                act.activation(ln_C[:, :], sd[:, 0, :], ACT.Copy, scale=1.0 / (CENTRE * P)).then_inc(*o.up(centre))

            def squares(layer, j, m):
                act.wait_ge(d_ready.sem, d_ready.val(layer, KD * j + m + 1))
                if m >= 2:
                    act.wait_ge(part_sums.sem, part_sums.val(layer, (POOLED - 1) * j + max(1, m - 2)))
                act.activation(ln_sq[m % 2][:, :], x[:, m, :], ACT.Square).then_inc(*o.up(sq_ready))

            def norm_tail(layer, j):
                act.activation(lut[:, :], ident[:, 0:1], ACT.Sqrt)
                squares(layer, j, 6)
                squares(layer, j, 7)
                act.wait_ge(var_ready.sem, var_ready.val(layer, j + 1))
                act.activation(tok[:, 3, :], tok[:, 2, :], ACT.Sqrt).then_inc(*o.up(root_ready))
                act.wait_ge(wide_ps.sem, wide_ps.val(layer, 2 * j + 1))
                act.activation(ln_M[:, :], sd[:, 0, :], ACT.Copy).then_inc(*o.up(mean_wide))
                c = PAR_LN + 16 * j + 8

                def stream(m):
                    act.wait_ge(x_ready.sem, x_ready.val(layer, KD * j + m + 1))
                    act.activation(x[:, m, :], x[:, m, :], ACT.Identity,
                                   bias=par[:, c + m:c + m + 1]).then_inc(*o.up(norm_ready))

                for m in range(KD):
                    act.wait_ge(scaled.sem, scaled.val(layer, KD * j + m + 1))
                    act.activation(xh[:, m, :], x[:, m, :], ACT.Identity,
                                   bias=par[:, c + m:c + m + 1]).then_inc(*o.up(xhi_ready))
                    if m:
                        stream(m - 1)
                stream(KD - 1)

            def ffn(layer, n0, f):
                with act.Fori(0, 11) as i:
                    o.enter(i, {w_hi: 4, silu_ready: 2, hid_h: 2})
                    split(layer, n0 + 1, it=i, per=2)
                    split(layer, n0 + 2, it=i, per=2)
                    act.wait_ge(slab_done.sem, slab_done.val(layer, n0 + 1) + i * 2)
                    act.wait_ge(hid_f.sem, hid_f.val(layer, 22 * f) + i * 2)
                    act.activation(sil[0][:, :], pm[0][:, :], ACT.Silu).then_inc(*o.up(silu_ready))
                    act.activation(sil[1][:, :], pm[1][:, :], ACT.Silu).then_inc(*o.up(silu_ready))
                    for m in range(2):
                        act.wait_ge(hid_f.sem, hid_f.val(layer, 22 * f + m + 1) + i * 2)
                        act.activation(hh[:, bass.ds(i * 2 + m, 1), :], hp[m][:, :].unsqueeze(1), ACT.Copy).then_inc(*o.up(hid_h))
                    o.leave(11)
                if f == 0:
                    act.wait_ge(kb_ready.sem, kb_ready.val(layer, 1))
                for p in range(4):
                    for t in range(3):
                        n = n0 + KF + 3 * p + t
                        split(layer, n + 1)
                        if (p, t) == (1, 0):
                            centre_copy(layer, 2 * f)
                        if (p, t) == (1, 2):
                            squares(layer, 2 * f, 0)
                            squares(layer, 2 * f, 1)
                    if p in (1, 2):
                        squares(layer, 2 * f, 2 * p)
                        squares(layer, 2 * f, 2 * p + 1)
                norm_tail(layer, 2 * f)

            def evacuate(layer, s):
                n = S_FFN + s
                par_ = n % 2
                act.wait_ge(slab_done.sem, slab_done.val(layer, n + 1))
                if s < 2:
                    outs = [(q[:, 2 * s + m, :], B_Q + 2 * s + m) for m in range(2)]
                elif s == 2:
                    outs = [(kT[:, :], B_K)]
                elif s == 3:
                    outs = [(vT[:, :], B_V)]
                elif s < 10:
                    dst = (mq, mk, mv)[(s - 4) // 2]
                    outs = [(dst[:, 2 * (s % 2) + m, :], B_MQ + 2 * (s - 4) + m) for m in range(2)]
                elif s < 18:
                    g = (s - 10) // 2
                    dst, b0 = ((cx, B_CX), (cc, B_CC), (cb, B_CB), (og, B_MO))[g]
                    outs = [(dst[:, 2 * (s % 2) + m, :], b0 + 2 * (s % 2) + m) for m in range(2)]
                if s == 16:
                    act.wait_ge(conv_u.sem, conv_u.val(layer, 4))
                for m, (dst, b) in enumerate(outs):
                    src = pm[2 * par_ + m][:, :]
                    if 6 <= s < 8:
                        act.activation(dst, src, ACT.Identity, bias=kbias[:, b - B_MK:b - B_MK + 1],
                                       scale=float(P) ** -0.5).then_inc(*o.up(proj))
                    else:
                        fn = ACT.Sigmoid if s >= 16 else ACT.Identity
                        act.activation(dst, src, fn, bias=par[:, b:b + 1]).then_inc(*o.up(proj))

            def memory_gates(layer, s):
                if s == 0:
                    act.wait_ge(gate_in.sem, gate_in.val(layer, 1))
                    act.activation(gs[:, :], gf[:, :], ACT.Abs).then_inc(*o.up(f_abs))
                    o.settle()
                    act.activation(gs[:, :], gs[:, :], ACT.Exp, scale=-1.0).then_inc(*o.up(f_exp))
                    act.wait_ge(f_one.sem, f_one.val(layer, 1))
                    act.activation(gs[:, :], gs[:, :], ACT.Ln).then_inc(*o.up(f_ln))
                if s == 4:
                    act.wait_ge(decay_row.sem, decay_row.val(layer, 1))
                    act.activation(mrow[0:1, 80:96], mrow[0:1, 64:80], ACT.Exp).then_inc(*o.up())
                    act.wait_ge(g_rows.sem, g_rows.val(layer, 1))
                    act.activation(rf[:, :], rg[:, :], ACT.Exp, bias=rz[:, 0:1], scale=-1.0).then_inc(*o.up())
                    act.activation(ri[:, :], rm[:, :], ACT.Exp, scale=-1.0).then_inc(*o.up())
                    act.activation(rb[:, :], ra[:, :], ACT.Exp, bias=rz[:, 1:2]).then_inc(*o.up(exp_rows))

            def attn_exp(layer, u):
                b = sx[u % 2]
                k0 = 128 if u < 2 else 0
                act.wait_ge(sc_max.sem, sc_max.val(layer, u + 1))
                for j in range(4):
                    act.activation(b[:, j, k0:256], b[:, j, k0:256], ACT.Exp, bias=nmx[:, j:j + 1],
                                   accum_out=sums[:, j:j + 1])
                act.activation(es[:, :], es[:, :], ACT.Exp).then_inc(*o.up(sc_exp))

            def attn_pT(layer, u):
                if u >= 2:
                    act.wait_ge(pT_ps.sem, pT_ps.val(layer, u + 1))
                    act.activation(pT[:, 0, :], sd[:, 2, :], ACT.Copy).then_inc(*o.up(pT_act))

            def attn_out(layer, u):
                blk, g = divmod(u, 2)
                act.wait_ge(o_ps.sem, o_ps.val(layer, u + 1))
                act.activation(yA[:, 2 * g:2 * g + 2, P * blk:P * blk + P],
                               sd[:, 2, 0:256].rearrange("p (a t) -> p a t", a=2), ACT.Copy).then_inc(*o.up(o_used))

            def mem1(layer, h):
                act.wait_ge(m1_ps.sem, m1_ps.val(layer, h + 1))
                act.activation(vt[:, :, :], sd[:, 3, :].rearrange("p (n t) -> p n t", n=NB), ACT.Copy).then_inc(*o.up(vt_ready))
                act.wait_ge(dm_ready.sem, dm_ready.val(layer, h + 1))
                for n in range(NB):
                    c = 4 * n + h
                    ins = act.activation(Dm[:, n, :], Dm[:, n, :], ACT.Exp, bias=cols[:, 0, c:c + 1])
                ins.then_inc(*o.up(dexp))

            def mem2(layer, h):
                act.wait_ge(m2_ps.sem, m2_ps.val(layer, h + 1))
                act.activation(numh[:, :, :], sd[:, 1, :].rearrange("p (n t) -> p n t", n=NB), ACT.Copy).then_inc(*o.up(numl_ready))

            def mem3(layer, h):
                act.wait_ge(mvar.sem, mvar.val(layer, h + 1))
                act.activation(rst[:, :], rst[:, :], ACT.Sqrt).then_inc(*o.up(mstd))

            def mem4(layer, h):
                act.wait_ge(ym_ready.sem, ym_ready.val(layer, h + 1))
                act.activation(yMh[:, h, :], ytmp[:, :], ACT.Copy).then_inc(*o.up(ym_hi))

            def mixer(layer):
                for s in range(S_MIX):
                    n = S_FFN + s
                    split(layer, n + 1)
                    if 7 <= s < 15:
                        attn_out(layer, s - 7)
                    if s >= 18 and s < 30:
                        h, r = divmod(s - 18, 3)
                        if r == 0:
                            mem1(layer, h)
                        if r == 1:
                            mem3(layer, h)
                        if r == 2:
                            mem4(layer, h)
                    if s < 18:
                        evacuate(layer, s)
                    elif s < 36:
                        t, r = divmod(s - 18, 3)
                        if r < 2:
                            act.wait_ge(slab_done.sem, slab_done.val(layer, n + 1))
                            for m in range(2):
                                b = B_G + 8 * BRANCH_ORDER[t // 2] + 4 * (t % 2) + 2 * r + m
                                if t > 0:
                                    act.wait_ge(prod.sem, prod.val(layer, 4 * (t - 1) + 2 * r + m + 1))
                                act.activation(gt[:, 2 * r + m, :], pm[2 * r + m][:, :], ACT.Sigmoid,
                                               bias=par[:, b:b + 1]).then_inc(*o.up(sig_ready))
                        elif t >= 4:
                            for m in range(4):
                                k = 4 * (t - 4) + m
                                act.wait_ge(merged.sem, merged.val(layer, k + 1))
                                act.activation(mh[k // 4][:, k % 4, :], x[:, k, :], ACT.Copy).then_inc(*o.up(mg_hi))
                    if s in (0, 4):
                        memory_gates(layer, s)
                    if 6 <= s < 14:
                        attn_pT(layer, s - 6)
                    if 5 <= s < 13:
                        attn_exp(layer, s - 5)
                    if s in (15, 16):
                        for c in (2 * (s - 15), 2 * (s - 15) + 1):
                            act.wait_ge(yc_f.sem, yc_f.val(layer, c + 1))
                            act.activation(yCh[:, c, :], convtmp[:, :], ACT.Copy).then_inc(*o.up(yc_hi))
                    if s == 23:
                        act.wait_ge(slab_done.sem, slab_done.val(layer, n + 1))
                        for c in range(4):
                            act.activation(yAh[:, c, :], yA[:, c, :], ACT.Copy).then_inc(*o.up(ya_hi))
                    if s >= 18 and s < 30 and (s - 18) % 3 == 0:
                        mem2(layer, (s - 18) // 3)
                    if s == 37:
                        centre_copy(layer, 1)
                        squares(layer, 1, 0)
                        squares(layer, 1, 1)
                    if s in (37, 38):
                        squares(layer, 1, 2 * (s - 36))
                        squares(layer, 1, 2 * (s - 36) + 1)
                norm_tail(layer, 1)

            start()
            with act.Fori(0, DEPTH) as layer:
                o.layer = layer
                ffn(layer, 0, 0)
                mixer(layer)
                ffn(layer, S_FFN + S_MIX, 1)
                o.done()

        @block.gpsimd
        def _(pool):
            o = Order(pool, own_pool)

            def norm(layer, j):
                S, Q = ln_S[:, :], ln_Q[:, :]
                pool.wait_ge(z_ready.sem, z_ready.val(layer, CENTRE * j + CENTRE))
                nc.gpsimd.tensor_tensor(S, x[:, 0, :], x[:, 1, :], ALU.add).then_inc(*o.up(z_sum))
                pool.wait_ge(centre_ps.sem, centre_ps.val(layer, j + 1))
                for m in range(1, POOLED):
                    pool.wait_ge(sq_ready.sem, sq_ready.val(layer, KD * j + m + 1))
                    first = (x[:, 0, :], ln_sq[0][:, :]) if m == 1 else (S, Q)
                    nc.gpsimd.tensor_tensor(S, first[0], x[:, m, :], ALU.add).then_inc(*o.up())
                    nc.gpsimd.tensor_tensor(Q, first[1], ln_sq[m % 2][:, :], ALU.add).then_inc(*o.up(part_sums))
                    o.settle()
                pool.wait_ge(mean_wide.sem, mean_wide.val(layer, j + 1))
                for m in range(1, KD):
                    nc.gpsimd.tensor_tensor(x[:, m, :], x[:, m, :], ln_M[:, :], ALU.subtract).then_inc(*o.up(cen_ready))

            with pool.Fori(0, DEPTH) as layer:
                o.layer = layer
                for j in range(3):
                    norm(layer, j)
                o.done()

        @block.vector
        def _(dve):
            o = Order(dve, own_dve)
            V = nc.vector
            steps = [0]

            def step(ins):
                ins.then_inc(setup.sem, 1)
                steps[0] += 1
                dve.wait_ge(setup.sem, steps[0])

            for t, sig in ((kbias, w_lo), (NS, w_lo), (mx, w_lo), (nmx, hid_f)):
                V.memset(t[:, :], 0.0).then_inc(sig.sem, 1)
            def split_half(layer, n, h, it=None, per=0):
                slot = n % 2
                v = w_hi.val(layer, 2 * n + h + 1)
                dve.wait_ge(w_hi.sem, v if it is None else v + it * 2 * per)
                for get, put in pieces(n, h):
                    ins = V.tensor_tensor(put(wl[slot]), get(raw[slot]), f32(put(wh[slot])), ALU.subtract)
                ins.then_inc(*o.up(w_lo))

            for h in range(2):
                split_half(0, 0, h)
                for k in range(4 * h, 4 * h + 4):
                    dve.wait_ge(xhi_ready.sem, k + 1)
                    V.tensor_tensor(xl[:, k, :], x[:, k, :], f32(xh[:, k, :]), ALU.subtract).then_inc(x_ready.sem, 1)
            dve.wait_ge(start_in.sem, 32)
            dve.wait_ge(pos_in.sem, 16)
            an, tu, co = mq[:, 0, :], mq[:, 1, :], mq[:, 2, :]
            step(V.tensor_copy(co, an.bitcast(I32)))
            step(V.tensor_scalar(an, co, const[:, K_FREQ:K_FREQ + 1], None, ALU.mult))
            step(V.tensor_scalar(tu, an, 1.0 / TWO_PI, None, ALU.mult))
            step(V.tensor_scalar(tu, tu, 12582912.0, None, ALU.add))
            step(V.tensor_scalar(tu, tu, -12582912.0, None, ALU.add))
            c1 = 6.28125
            c2 = float(np.float32(np.floor((TWO_PI - c1) * 2**20) / 2**20))
            for c in (c1, c2, TWO_PI - c1 - c2):
                step(V.scalar_tensor_tensor(out=an, in0=tu, scalar=-c, in1=an, op0=ALU.mult, op1=ALU.add))
            step(V.tensor_scalar(an, an, 3.1415925, -3.1415925, ALU.min, ALU.max))
            step(V.scalar_tensor_tensor(out=tu, in0=an, scalar=-1.0, in1=an, op0=ALU.mult, op1=ALU.max))
            step(V.tensor_scalar(tu, tu, -1.0, float(np.pi / 2), ALU.mult, ALU.add))
            assert steps[0] == SETUP_STEPS

            def split(layer, n, it=None, per=0):
                for h in range(2):
                    split_half(layer, n, h, it, per)

            def stream_times_alpha(layer, j, m, add, op, sig):
                if j != 1:
                    V.scalar_tensor_tensor(out=x[:, m, :], in0=x[:, m, :], scalar=ALPHA, in1=add,
                                           op0=ALU.mult, op1=op).then_inc(*o.up(sig))
                else:
                    V.scalar_tensor_tensor(out=x[:, m, :], in0=f32(xh[:, m, :]), scalar=ALPHA, in1=add,
                                           op0=ALU.mult, op1=op).then_inc(*o.up())
                    o.settle()
                    V.scalar_tensor_tensor(out=x[:, m, :], in0=f32(xl[:, m, :]), scalar=ALPHA, in1=x[:, m, :],
                                           op0=ALU.mult, op1=ALU.add).then_inc(*o.up(sig))

            def outputs(layer, j, p, done):
                if p == 3:
                    dve.wait_ge(seventh_ps.sem, seventh_ps.val(layer, j + 1))
                else:
                    dve.wait_ge(slab_done.sem, done)
                for m in (2 * p, 2 * p + 1):
                    bank = 2 * (p % 2) + m % 2
                    if m == 7:
                        dve.wait_ge(slab_done.sem, done)
                    if p == 0:
                        stream_times_alpha(layer, j, m, pm[bank][:, :], ALU.add, z_ready)
                    else:
                        V.tensor_tensor(x[:, m, :], x[:, m, :], pm[bank][:, :], ALU.add).then_inc(*o.up(d_ready))
                    if m == 6:
                        dve.wait_ge(part_sums.sem, part_sums.val(layer, (POOLED - 1) * (j + 1)))
                        o.settle()
                        V.tensor_tensor(ln_S[:, :], ln_S[:, :], x[:, m, :], ALU.add).then_inc(*o.up())
                        dve.wait_ge(sq_ready.sem, sq_ready.val(layer, KD * j + m + 1))
                        V.scalar_tensor_tensor(out=ln_Q[:, :], in0=ln_sq[0][:, :], scalar=EPS * KD, in1=ln_Q[:, :],
                                               op0=ALU.add, op1=ALU.add).then_inc(*o.up(sums_ready))

            def centre_all(layer, j):
                dve.wait_ge(centre.sem, centre.val(layer, j + 1))
                for m in range(CENTRE):
                    V.tensor_tensor(x[:, m, :], x[:, m, :], ln_C[:, :], ALU.subtract).then_inc(*o.up(d_ready))
                for m in range(CENTRE, KD):
                    stream_times_alpha(layer, j, m, ln_C[:, :], ALU.subtract, None)
                o.settle()

            def norm_tail(layer, j):
                mean, square, var, dev, inv = (tok[:, i, :] for i in range(5))

                def diagonal(dst, v):
                    V.tensor_tensor(dst[:, :].rearrange("p (n t) -> p n t", n=NB),
                                    ident.unsqueeze(1).broadcast_to([P, NB, P]),
                                    v.unsqueeze(2).broadcast_to([P, NB, P]), ALU.mult).then_inc(*o.up(diag_ready))

                dve.wait_ge(stat_ps.sem, stat_ps.val(layer, 2 * j + 1))
                V.tensor_scalar(mean, sd[:, 2, 0:NB], 1.0 / D, None, ALU.mult).then_inc(*o.up())
                o.settle()
                V.tensor_tensor(square, mean, mean, ALU.mult).then_inc(*o.up())
                o.settle()
                dve.wait_ge(stat_ps.sem, stat_ps.val(layer, 2 * j + 2))
                apart(dve)
                V.scalar_tensor_tensor(out=var, in0=sd[:, 3, 0:NB], scalar=1.0 / D, in1=square,
                                       op0=ALU.mult, op1=ALU.subtract).then_inc(*o.up(var_ready))
                diagonal(ln_S, mean)
                dve.wait_ge(root_ready.sem, root_ready.val(layer, j + 1))
                V.reciprocal(inv, dev).then_inc(*o.up())
                o.settle()
                diagonal(ln_Q, inv)
                dve.wait_ge(mean_wide.sem, mean_wide.val(layer, j + 1))
                V.tensor_tensor(x[:, 0, :], x[:, 0, :], ln_M[:, :], ALU.subtract).then_inc(*o.up())
                o.settle()
                dve.wait_ge(wide_ps.sem, wide_ps.val(layer, 2 * j + 2))
                c = PAR_LN + 16 * j

                def low(m):
                    dve.wait_ge(xhi_ready.sem, xhi_ready.val(layer, KD * j + m + 1))
                    V.scalar_tensor_tensor(out=xl[:, m, :], in0=x[:, m, :], scalar=par[:, c + 8 + m:c + 9 + m],
                                           in1=f32(xh[:, m, :]), op0=ALU.add, op1=ALU.subtract).then_inc(*o.up(x_ready))

                for m in range(KD):
                    if m:
                        dve.wait_ge(cen_ready.sem, cen_ready.val(layer, (KD - 1) * j + m))
                    V.scalar_tensor_tensor(out=x[:, m, :], in0=x[:, m, :], scalar=par[:, c + m:c + m + 1],
                                           in1=sd[:, 1, :], op0=ALU.mult, op1=ALU.mult).then_inc(*o.up(scaled))
                    if m:
                        low(m - 1)
                low(KD - 1)

            def ffn(layer, n0, f):
                with dve.Fori(0, 11) as i:
                    o.enter(i, {w_lo: 4, hid_f: 2, hid_l: 2})
                    split(layer, n0 + 1, it=i, per=2)
                    split(layer, n0 + 2, it=i, per=2)
                    dve.wait_ge(slab_done.sem, slab_done.val(layer, n0 + 2) + i * 2)
                    for m in range(2):
                        dve.wait_ge(silu_ready.sem, silu_ready.val(layer, 22 * f + m + 1) + i * 2)
                        V.scalar_tensor_tensor(out=hp[m][:, :], in0=pm[2 + m][:, :], scalar=0.5, in1=sil[m][:, :],
                                               op0=ALU.mult, op1=ALU.mult).then_inc(*o.up(hid_f))
                    for m in range(2):
                        dve.wait_ge(hid_h.sem, hid_h.val(layer, 22 * f + m + 1) + i * 2)
                        c = bass.ds(i * 2 + m, 1)
                        V.tensor_tensor(hl[:, c, :], hp[m][:, :].unsqueeze(1), f32(hh[:, c, :]),
                                        ALU.subtract).then_inc(*o.up(hid_l))
                    o.leave(11)
                if f == 0:
                    dve.wait_ge(start_in.sem, 32)
                    dve.wait_ge(norm_ready.sem, norm_ready.val(layer, 0))
                    V.tensor_copy(par[:, :].unsqueeze(1), par_all[:, bass.ds(layer, 1), :]).then_inc(*o.up(par_ready))
                    o.settle()
                    V.tensor_scalar(kbias[:, :], par[:, B_MK:B_MK + 4], float(P) ** -0.5, None,
                                    ALU.mult).then_inc(*o.up(kb_ready))
                for p in range(4):
                    for t in range(3):
                        n = n0 + KF + 3 * p + t
                        split(layer, n + 1)
                        if (p, t) == (1, 0):
                            centre_all(layer, 2 * f)
                    if p == 0:
                        dve.wait_ge(norm_ready.sem, norm_ready.val(layer, 2 * KD * f))
                    outputs(layer, 2 * f, p, slab_done.val(layer, n + 1))
                norm_tail(layer, 2 * f)

            def rope(layer, r, t, bank):
                dve.wait_ge(rot_ps.sem, rot_ps.val(layer, r + 1))
                V.tensor_tensor(ropetmp[:, :], sd[:, bank, :], sinT[:, :], ALU.mult).then_inc(*o.up(rot_used))
                V.tensor_tensor(t, t, cosT[:, :], ALU.mult).then_inc(*o.up())
                o.settle()
                V.tensor_tensor(t, t, ropetmp[:, :], ALU.add).then_inc(*o.up(roped))
                o.settle()

            def memory_gates(layer, s):
                if s == 0:
                    dve.wait_ge(gate_ps.sem, gate_ps.val(layer, 1))
                    g = sd[:, 3, 0:32].rearrange("p (n g) -> p n g", g=8)
                    for dst, c in ((gi, 0), (gf, 4)):
                        bias = par[:, PAR_IF + c:PAR_IF + c + 4].unsqueeze(1).broadcast_to([P, NB, 4])
                        ins = V.tensor_tensor(dst[:, :].rearrange("p (n h) -> p n h", h=4), g[:, :, c:c + 4], bias, ALU.add)
                    ins.then_inc(*o.up(gate_in))
                    dve.wait_ge(f_exp.sem, f_exp.val(layer, 1))
                    V.tensor_scalar(gs[:, :], gs[:, :], 1.0, None, ALU.add).then_inc(*o.up(f_one))
                    dve.wait_ge(f_ln.sem, f_ln.val(layer, 1))
                    V.scalar_tensor_tensor(out=gf[:, :], in0=gf[:, :], scalar=0.0, in1=gs[:, :],
                                           op0=ALU.min, op1=ALU.subtract).then_inc(*o.up(gates_tok))
                if s == 2:
                    dve.wait_ge(rows_ps.sem, rows_ps.val(layer, 1))
                    V.tensor_copy(rf[:, :], sd[0:16, 2, 0:128])
                    V.tensor_copy(ri[:, :], sd[0:16, 2, 128:256])
                    V.memset(rz[:, :], 0.0).then_inc(*o.up())
                    o.settle()
                    V.tensor_tensor_scan(rb[:, :], rf[:, :], rz[:, :], 0.0, ALU.add, ALU.add).then_inc(*o.up())
                    o.settle()
                    V.tensor_tensor(ra[:, :], ri[:, :], rb[:, :], ALU.subtract).then_inc(*o.up())
                    o.settle()
                    V.tensor_tensor_scan(rloc[:, :], ra[:, :], ra[:, :], -3e38, ALU.max, ALU.max).then_inc(*o.up(scans))
                if s == 3:
                    dve.wait_ge(ends_ps.sem, ends_ps.val(layer, 1))
                    V.tensor_copy(mrow[0:1, 0:32], sd[0:1, 2, 256:288])
                    V.memset(mrow[0:1, 32:36], 0.0).then_inc(*o.up())
                    for n in range(NB):
                        o.settle()
                        a, b, m, g = (mrow[0:1, c + 4 * n:c + 4 * n + 4] for c in (16, 0, 32, 48))
                        V.tensor_tensor(g, m, a, ALU.max).then_inc(*o.up(carry if n == NB - 1 else None))
                        o.settle()
                        if n < NB - 1:
                            V.tensor_tensor(mrow[0:1, 36 + 4 * n:40 + 4 * n], b, g, ALU.add).then_inc(*o.up())
                    V.tensor_tensor(mrow[0:1, 64:80], mrow[0:1, 32:48], mrow[0:1, 48:64], ALU.subtract).then_inc(*o.up(decay_row))
                if s == 4:
                    dve.wait_ge(carry_ps.sem, carry_ps.val(layer, 1))
                    V.tensor_copy(rz[:, 0:1], sd[0:16, 2, 300:301])
                    V.tensor_scalar(rz[:, 1:2], sd[0:16, 2, 301:302], -1.0, None, ALU.mult).then_inc(*o.up())
                    o.settle()
                    V.tensor_scalar(rg[:, :], rloc[:, :], rz[:, 0:1], None, ALU.max).then_inc(*o.up())
                    o.settle()
                    V.tensor_tensor(rm[:, :], rb[:, :], rg[:, :], ALU.add).then_inc(*o.up(g_rows))
                if s == 5:
                    dve.wait_ge(cols_ps.sem, cols_ps.val(layer, 1))
                    V.tensor_copy(cols[:, :, :], sd[:, 3, 0:80].rearrange("p (a b) -> p a b", a=5)).then_inc(*o.up(cols_ready))

            def attn_scores(layer, u):
                b, g = sx[u % 2], u % 2
                k0 = 128 if u < 2 else 0
                dve.wait_ge(sc_ps.sem, sc_ps.val(layer, u + 1))
                s4 = sd[:, 0:2, :].rearrange("p b (j k) -> p (b j) k", j=2)
                mask = const[:, K_MASK + k0:K_MASK + 256].unsqueeze(1).broadcast_to([P, 4, 256 - k0])
                V.scalar_tensor_tensor(out=b[:, :, k0:256], in0=s4[:, :, k0:256], scalar=float(HD) ** -0.5,
                                       in1=mask, op0=ALU.mult, op1=ALU.add).then_inc(*o.up())
                o.settle()
                V.tensor_reduce(mx[:, :], b[:, :, k0:256], AX.X, ALU.max).then_inc(*o.up())
                o.settle()
                sink = par[:, PAR_SINK + 4 * g:PAR_SINK + 4 * g + 4]
                V.tensor_tensor(mx[:, :], mx[:, :], sink, ALU.max).then_inc(*o.up())
                o.settle()
                V.tensor_tensor(es[:, :], sink, mx[:, :], ALU.subtract)
                V.tensor_scalar(nmx[:, :], mx[:, :], -1.0, None, ALU.mult).then_inc(*o.up(sc_max))

            def attn_norm(layer, u):
                b = sx[u % 2]
                k0 = 128 if u < 2 else 0
                dve.wait_ge(sc_exp.sem, sc_exp.val(layer, u + 1))
                V.tensor_tensor(sums[:, :], sums[:, :], es[:, :], ALU.add).then_inc(*o.up())
                o.settle()
                V.reciprocal(mx[:, :], sums[:, :]).then_inc(*o.up())
                o.settle()
                V.tensor_tensor(b[:, :, k0:256], b[:, :, k0:256], mx[:, :].unsqueeze(2).broadcast_to([P, 4, 256 - k0]),
                                ALU.mult).then_inc(*o.up(p_ready))

            def attn_pT(layer, u):
                dve.wait_ge(pT_ps.sem, pT_ps.val(layer, u + 1))
                V.tensor_copy(pT[:, 1, :], sd[:, 3, :]).then_inc(*o.up(pT_dve))

            def row_of(layer, h):
                hm = const[0:16, K_HM + 4 * h:K_HM + 4 * h + 4].unsqueeze(2).broadcast_to([16, NB, P])
                V.tensor_tensor(rowx[:, :, :], rg[:, :].unsqueeze(1).broadcast_to([16, NB, P]), hm,
                                ALU.mult).then_inc(*o.up(rowx_ready))

            def of_head(kind, h):
                return cols[:, kind, :].rearrange("p (n h) -> p n h", h=4)[:, :, h]

            def n4(a):
                return a.rearrange("p (n t) -> p n t", n=NB)

            def mem1(layer, h):
                dve.wait_ge(m1_ps.sem, m1_ps.val(layer, h + 1))
                mt = const[:, K_MT:K_MT + P].unsqueeze(1).broadcast_to([P, NB, P])
                V.scalar_tensor_tensor(out=Dm[:, :, :], in0=n4(sd[:, 1, :]), scalar=-1.0, in1=mt,
                                       op0=ALU.mult, op1=ALU.add).then_inc(*o.up(dm_ready))
                V.tensor_tensor(kw[:, :, :], n4(sd[:, 2, :]), of_head(3, h).unsqueeze(2).broadcast_to([P, NB, P]),
                                ALU.mult).then_inc(*o.up())
                dve.wait_ge(dexp.sem, dexp.val(layer, h + 1))
                V.tensor_tensor(Dm[:, :, :], Dm[:, :, :], n4(sd[:, 0, :]), ALU.mult).then_inc(*o.up(s_ready))

            def mem2(layer, h):
                dve.wait_ge(m2_ps.sem, m2_ps.val(layer, h + 1))
                V.tensor_copy(CS[:, 0, :], sd[:, 2, 0:P])
                V.tensor_copy(NS[:, 0:1], sd[:, 3, 8:9]).then_inc(*o.up())
                for n in (1, 2):
                    o.settle()
                    dec = cols[:, 4, 4 * n + h:4 * n + h + 1]
                    V.scalar_tensor_tensor(out=CS[:, n, :], in0=CS[:, n - 1, :], scalar=dec,
                                           in1=sd[:, 2, P * n:P * n + P], op0=ALU.mult, op1=ALU.add)
                    V.scalar_tensor_tensor(out=NS[:, n:n + 1], in0=NS[:, n - 1:n], scalar=dec,
                                           in1=sd[:, 3, 8 + n:9 + n], op0=ALU.mult,
                                           op1=ALU.add).then_inc(*o.up(st_ready if n == 2 else None))

            def mem3(layer, h):
                dve.wait_ge(m3_ps.sem, m3_ps.val(layer, h + 1))
                dve.wait_ge(numl_ready.sem, numl_ready.val(layer, h + 1))
                V.tensor_copy(dn[:, 0:4], sd[:, 3, 0:4])
                V.tensor_copy(dn[:, 5:8], sd[:, 3, 5:8]).then_inc(*o.up())
                for n in (1, 2, 3):
                    w = cols[:, 1, 4 * n + h:4 * n + h + 1]
                    V.scalar_tensor_tensor(out=numh[:, n, :], in0=sd[:, 0, P * n:P * n + P], scalar=w,
                                           in1=numh[:, n, :], op0=ALU.mult, op1=ALU.add).then_inc(*o.up())
                o.settle()
                V.tensor_tensor(dn[:, 5:8], dn[:, 5:8], of_head(1, h)[:, 1:4], ALU.mult).then_inc(*o.up())
                o.settle()
                V.tensor_tensor(dens[:, 1:4], dn[:, 5:8], dn[:, 1:4], ALU.add)
                V.tensor_copy(dens[:, 0:1], dn[:, 0:1]).then_inc(*o.up())
                o.settle()
                V.scalar_tensor_tensor(out=nden[:, :], in0=dens[:, :], scalar=-1.0, in1=dens[:, :],
                                       op0=ALU.mult, op1=ALU.max).then_inc(*o.up())
                o.settle()
                V.tensor_tensor(nden[:, :], nden[:, :], of_head(2, h), ALU.max).then_inc(*o.up())
                o.settle()
                V.reciprocal(dens[:, :], nden[:, :]).then_inc(*o.up())
                o.settle()
                V.tensor_tensor(numh[:, :, :], numh[:, :, :], dens[:, :].unsqueeze(2).broadcast_to([P, NB, P]),
                                ALU.mult).then_inc(*o.up())
                o.settle()
                for n in range(NB):
                    V.bn_stats(bst[:, n, :], numh[:, n, :]).then_inc(*o.up())
                o.settle()
                apart(dve)
                for n in range(NB):
                    V.bn_aggr(bag[:, n, :], bst[:, n, :]).then_inc(*o.up())
                o.settle()
                V.tensor_scalar(rst[:, :], bag[:, :, 1], EPS, None, ALU.add).then_inc(*o.up(mvar))
                dve.wait_ge(mstd.sem, mstd.val(layer, h + 1))
                V.reciprocal(dens[:, :], rst[:, :]).then_inc(*o.up())
                o.settle()
                for n in range(NB):
                    ins = V.tensor_scalar(numh[:, n, :], numh[:, n, :], bag[:, n, 0:1], dens[:, n:n + 1],
                                          ALU.subtract, ALU.mult)
                ins.then_inc(*o.up(hn_ready))

            def mem4(layer, h):
                dve.wait_ge(m4_ps.sem, m4_ps.val(layer, h + 1))
                V.scalar_tensor_tensor(out=ytmp[:, :], in0=sd[:, 0, :], scalar=par[:, PAR_NW + h:PAR_NW + h + 1],
                                       in1=og[:, h, :], op0=ALU.mult, op1=ALU.mult).then_inc(*o.up(ym_ready))
                dve.wait_ge(ym_hi.sem, ym_hi.val(layer, h + 1))
                V.tensor_tensor(yMl[:, h, :], ytmp[:, :], f32(yMh[:, h, :]), ALU.subtract).then_inc(*o.up(ym_lo))

            def conv(layer, c):
                w = [par[:, PAR_CONV + 4 * k + c:PAR_CONV + 4 * k + c + 1] for k in range(3)]
                u, y = cx[:, c, :], convtmp[:, :]
                V.tensor_scalar(y, u, w[2], None, ALU.mult).then_inc(*o.up())
                for k in (1, 0):
                    o.settle()
                    d = 2 - k
                    V.scalar_tensor_tensor(out=y[:, d:], in0=u[:, :SEQ - d], scalar=w[k], in1=y[:, d:],
                                           op0=ALU.mult, op1=ALU.add).then_inc(*o.up())
                o.settle()
                V.tensor_tensor(y, y, cb[:, c, :], ALU.mult).then_inc(*o.up(yc_f))
                dve.wait_ge(yc_hi.sem, yc_hi.val(layer, c + 1))
                V.tensor_tensor(yCl[:, c, :], y, f32(yCh[:, c, :]), ALU.subtract).then_inc(*o.up(yc_lo))
                o.settle()

            def branch(layer, t):
                for m in range(4):
                    k = 4 * (t % 2) + m
                    if m < 3:
                        dve.wait_ge(br_ps.sem, br_ps.val(layer, 3 * t + m + 1))
                    else:
                        dve.wait_ge(slab_done.sem, slab_done.val(layer, S_FFN + 18 + 3 * t + 3))
                    dve.wait_ge(sig_ready.sem, sig_ready.val(layer, 4 * t + m + 1))
                    dst = x[:, k, :] if t < 2 else mtmp[:, :]
                    V.tensor_tensor(dst, pm[m][:, :], gt[:, m, :], ALU.mult).then_inc(*o.up(prod))
                    if t >= 2:
                        o.settle()
                        V.tensor_tensor(x[:, k, :], x[:, k, :], mtmp[:, :], ALU.add).then_inc(*o.up(merged if t >= 4 else None))
                        o.settle()
                    if t >= 4:
                        dve.wait_ge(mg_hi.sem, mg_hi.val(layer, k + 1))
                        V.tensor_tensor(ml[k // 4][:, k % 4, :], x[:, k, :], f32(mh[k // 4][:, k % 4, :]),
                                        ALU.subtract).then_inc(*o.up(mg_lo))

            def projected(layer, s):
                dve.wait_ge(proj.sem, proj.val(layer, proj_count(s)))

            def mixer(layer):
                for s in range(S_MIX):
                    n = S_FFN + s
                    split(layer, n + 1)
                    h, r = divmod(s - 18, 3)
                    if s in (2, 3, 4, 5):
                        memory_gates(layer, s)
                    if 18 <= s < 30:
                        (mem1, mem3, mem4)[r](layer, h)
                    if s == 0:
                        memory_gates(layer, s)
                        dve.wait_ge(table_ready.sem, 2)
                    if s == 1:
                        rope(layer, 0, q[:, 0, :], 0)
                        rope(layer, 1, q[:, 1, :], 1)
                    if s == 2:
                        rope(layer, 2, q[:, 2, :], 0)
                        rope(layer, 3, q[:, 3, :], 1)
                    if s == 3:
                        rope(layer, 4, kT[:, :], 0)
                    if s == 4:
                        dve.wait_ge(v_ps.sem, v_ps.val(layer, 1))
                        V.tensor_copy(vtok[:, :, :], n4(sd[:, 1, :])).then_inc(*o.up(v_ready))
                    if 6 <= s < 14:
                        attn_pT(layer, s - 6)
                    if 5 <= s < 13:
                        attn_scores(layer, s - 5)
                        attn_norm(layer, s - 5)
                    if s == 13:
                        projected(layer, s)
                        for c in range(4):
                            V.tensor_tensor(cx[:, c, :], cx[:, c, :], cc[:, c, :], ALU.mult).then_inc(*o.up(conv_u))
                        o.settle()
                    if s in (15, 16):
                        projected(layer, s - 1)
                        for c in (2 * (s - 15), 2 * (s - 15) + 1):
                            conv(layer, c)
                    if s == 17:
                        projected(layer, s)
                        row_of(layer, 0)
                    if 18 <= s < 30 and r == 0:
                        mem2(layer, h)
                    if 18 <= s < 27 and r == 2:
                        row_of(layer, h + 1)
                    if 18 <= s < 36 and r == 2:
                        branch(layer, h)
                    if s == 23:
                        for c in range(4):
                            dve.wait_ge(ya_hi.sem, ya_hi.val(layer, c + 1))
                            V.tensor_tensor(yAl[:, c, :], yA[:, c, :], f32(yAh[:, c, :]), ALU.subtract).then_inc(*o.up(ya_lo))
                    if s >= 36:
                        if s == 37:
                            centre_all(layer, 1)
                        outputs(layer, 1, s - 36, slab_done.val(layer, n + 1))
                norm_tail(layer, 1)

            with dve.Fori(0, DEPTH) as layer:
                o.layer = layer
                ffn(layer, 0, 0)
                mixer(layer)
                ffn(layer, S_FFN + S_MIX, 1)
                o.done()

        @block.tensor
        def _(pe):
            T = nc.tensor

            def slab(layer, n, banks, rh, rl, k_first=0, starts=True, stops=True, it=None, per=0,
                     before_k=None, before_m=None, middle=None, between=None):
                kk, cw = slab_shape(n)
                slot = n % 2
                W, L_ = (w[slot][:, 0:kk * cw].rearrange("p (k c) -> p k c", c=cw) for w in (wh, wl))
                kh = half(n, 1)[0] // cw
                ms = range(len(banks))
                order = [(k, m) for m in ms for k in range(kk)] if between else [(k, m) for k in range(kk) for m in ms]
                seen = set()
                for k, m in order:
                    if (k >= kh) not in seen:
                        seen.add(k >= kh)
                        v = w_lo.val(layer, 2 * n + (2 if k >= kh else 1))
                        pe.wait_ge(w_lo.sem, v if it is None else v + it * 2 * per)
                        if k >= kh and middle is not None:
                            middle()
                    if before_m is not None and k == 0:
                        before_m(m)
                    if before_k is not None and (k, "k") not in seen:
                        seen.add((k, "k"))
                        before_k(k_first + k)
                    hi, lo = W[:, k, P * m:P * m + P], L_[:, k, P * m:P * m + P]
                    out = pm[banks[m]][:, :]
                    a, b = rh(k_first + k), rl(k_first + k)
                    T.matmul(out, hi, a, start=starts and k == 0, stop=False)
                    T.matmul(out, hi, b, start=False, stop=False)
                    ins = T.matmul(out, lo, a, start=False, stop=stops and k == kk - 1)
                    if between and k == kk - 1 and m < len(banks) - 1:
                        ins.then_inc(between.sem, 1)
                ins.then_inc(slab_done.sem, 1)

            def xhk(k):
                return xh[:, k, :]

            def xlk(k):
                return xl[:, k, :]

            def stream_wait(layer, c):
                def wait(k):
                    pe.wait_ge(x_ready.sem, x_ready.val(layer, KD * (c - 1) + k + 1))
                return wait

            def centre_sum(layer, j):
                pe.wait_ge(z_sum.sem, z_sum.val(layer, j + 1))
                T.matmul(sd[:, 0, :], ones, ln_S[:, :], start=True, stop=True).then_inc(centre_ps.sem, 1)

            def stat_sums(layer, j):
                def add(bank, t, first):
                    for n in range(NB):
                        ins = T.matmul(sd[:, bank, n:n + 1], t[:, P * n:P * n + P], ones[:, 0:1],
                                       start=first and n == 0, stop=not first, skip_group_check=True)
                    return ins

                pe.wait_ge(sums_ready.sem, sums_ready.val(layer, j + 1))
                add(2, ln_S, True)
                add(3, ln_Q, True)
                pe.wait_ge(d_ready.sem, d_ready.val(layer, KD * j + KD))
                add(2, x[:, 7, :], False).then_inc(stat_ps.sem, 1)
                pe.wait_ge(sq_ready.sem, sq_ready.val(layer, KD * j + KD))
                add(3, ln_sq[1], False).then_inc(stat_ps.sem, 1)
                for i, t in enumerate((ln_S, ln_Q)):
                    pe.wait_ge(diag_ready.sem, diag_ready.val(layer, 2 * j + i + 1))
                    T.matmul(sd[:, i, :], ones, t[:, :], start=True, stop=True).then_inc(wide_ps.sem, 1)

            def ffn(layer, n0, f):
                with pe.Fori(0, 11) as i:
                    pe.wait_ge(silu_ready.sem, silu_ready.val(layer, 22 * f) + i * 2)
                    slab(layer, n0, (0, 1), xhk, xlk, it=i, per=2, before_k=stream_wait(layer, 2 * f))
                    pe.wait_ge(hid_f.sem, hid_f.val(layer, 22 * f) + i * 2)
                    slab(layer, n0 + 1, (2, 3), xhk, xlk, it=i, per=2)

                def hidden(k):
                    pe.wait_ge(hid_l.sem, hid_l.val(layer, 22 * f + k + 1))

                for p in range(4):
                    if p == 0:
                        pe.wait_ge(silu_ready.sem, silu_ready.val(layer, 22 * f + 22))
                    elif p == 1:
                        pe.wait_ge(hid_f.sem, hid_f.val(layer, 22 * f + 22))
                    elif p == 2:
                        pe.wait_ge(z_ready.sem, z_ready.val(layer, 2 * f * CENTRE + 2))
                    else:
                        pe.wait_ge(d_ready.sem, d_ready.val(layer, 2 * f * KD + 4))
                    for t in range(3):
                        slab(layer, n0 + KF + 3 * p + t, (2 * (p % 2), 2 * (p % 2) + 1),
                             lambda k: hh[:, k, :], lambda k: hl[:, k, :], k_first=8 * t, starts=t == 0, stops=t == 2,
                             before_k=hidden if p == 0 else None,
                             middle=(lambda: centre_sum(layer, 2 * f)) if (p, t) == (1, 0) else None,
                             between=seventh_ps if (p, t) == (3, 2) else None)
                stat_sums(layer, 2 * f)

            def gate_products(layer):
                pe.wait_ge(wif_in.sem, wif_in.val(layer, 16))
                pe.wait_ge(norm_ready.sem, norm_ready.val(layer, KD))
                for n in range(NB):
                    for k in range(KD):
                        ins = T.matmul(sd[:, 3, 8 * n:8 * n + 8], x[:, k, P * n:P * n + P], wif[:, k, :],
                                       start=k == 0, stop=k == KD - 1)
                ins.then_inc(gate_ps.sem, 1)

            def rotate(layer, r, t, bank, s):
                pe.wait_ge(proj.sem, proj.val(layer, proj_count(s)))
                if r >= 2:
                    pe.wait_ge(rot_used.sem, rot_used.val(layer, r - 1))
                T.matmul(sd[:, bank, :], const[:, K_ROT:K_ROT + P], t, start=True, stop=True).then_inc(rot_ps.sem, 1)

            def middle_job(layer, s):
                if s == 2:
                    pe.wait_ge(gates_tok.sem, gates_tok.val(layer, 1))
                    T.transpose(sd[0:16, 2, 0:128], gf[:, :], ident)
                    T.transpose(sd[0:16, 2, 128:256], gi[:, :], ident).then_inc(rows_ps.sem, 1)
                if s == 3:
                    pe.wait_ge(scans.sem, scans.val(layer, 1))
                    apart(pe)
                    T.transpose(sd[0:1, 2, 256:272], rb[:, 127:128], ident[0:16, 0:16])
                    T.transpose(sd[0:1, 2, 272:288], rloc[:, 127:128], ident[0:16, 0:16]).then_inc(ends_ps.sem, 1)
                if s == 4:
                    pe.wait_ge(carry.sem, carry.val(layer, 1))
                    apart(pe)
                    T.transpose(sd[0:16, 2, 300:301], mrow[0:1, 32:48], ident[0:1, 0:1])
                    T.transpose(sd[0:16, 2, 301:302], mrow[0:1, 48:64], ident[0:1, 0:1]).then_inc(carry_ps.sem, 1)
                if s == 5:
                    pe.wait_ge(exp_rows.sem, exp_rows.val(layer, 1))
                    apart(pe)
                    for i, row in enumerate((ra, rf, ri, rb)):
                        T.transpose(sd[:, 3, 16 * i:16 * i + 16], row[:, :], ident[0:16, 0:16])
                    T.matmul(sd[:, 3, 64:80], ones[0:1, :], mrow[0:1, 80:96], start=True, stop=True).then_inc(cols_ps.sem, 1)
                if 18 <= s < 30:
                    h, r = divmod(s - 18, 3)
                    if r == 0:
                        if h == 0:
                            pe.wait_ge(o_used.sem, o_used.val(layer, 8))
                            pe.wait_ge(pT_dve.sem, pT_dve.val(layer, 8))
                            pe.wait_ge(proj.sem, proj.val(layer, proj_count(9)))
                        else:
                            pe.wait_ge(ym_ready.sem, ym_ready.val(layer, h))
                        pe.wait_ge(rowx_ready.sem, rowx_ready.val(layer, h + 1))
                        T.matmul(sd[:, 1, :], ones[0:16, :], rowx[:, :, :].rearrange("p n t -> p (n t)"), start=True, stop=True)
                        for n in range(NB):
                            c = slice(P * n, P * n + P)
                            T.matmul(sd[:, 0, c], mk[:, h, c], mq[:, h, c], start=True, stop=True)
                        for n in range(NB):
                            c = slice(P * n, P * n + P)
                            T.transpose(sd[:, 2, c], mk[:, h, c], ident)
                        for n in range(NB):
                            c = slice(P * n, P * n + P)
                            ins = T.transpose(sd[:, 3, c], mv[:, h, c], ident)
                        ins.then_inc(m1_ps.sem, 1)
                    if r == 1:
                        pe.wait_ge(st_ready.sem, st_ready.val(layer, h + 1))
                        for n in (1, 2, 3):
                            c = slice(P * n, P * n + P)
                            T.matmul(sd[:, 0, c], mq[:, h, c], CS[:, n - 1, :], start=True, stop=True)
                            ins = T.matmul(sd[:, 3, 4 + n:5 + n], mq[:, h, c], NS[:, n - 1:n], start=True, stop=True)
                        ins.then_inc(m3_ps.sem, 1)
                    if r == 2:
                        pe.wait_ge(hn_ready.sem, hn_ready.val(layer, h + 1))
                        for n in range(NB):
                            ins = T.transpose(sd[:, 0, P * n:P * n + P], numh[:, n, :], ident)
                        ins.then_inc(m4_ps.sem, 1)
                if 7 <= s < 15:
                    u = s - 7
                    blk, g = divmod(u, 2)
                    pe.wait_ge(pT_dve.sem, pT_dve.val(layer, u + 1))
                    if u >= 2:
                        pe.wait_ge(pT_act.sem, pT_act.val(layer, u - 1))
                    ws = (0, 1) if u >= 2 else (1,)
                    for par_ in range(2):
                        for w in ws:
                            rhs = pT[:, w, :].rearrange("p (a b t) -> p a b t", a=2, b=2)[:, :, par_, :]
                            ins = T.matmul(sd[HD * par_:HD * par_ + HD, 2, 0:256].rearrange("p (a t) -> p a t", a=2),
                                           vtok[:, blk - 1 + w, HD * g:HD * g + HD], rhs, start=w == ws[0], stop=w == 1)
                    ins.then_inc(o_ps.sem, 1)
                if s == 37:
                    centre_sum(layer, 1)

            def end_job(layer, s):
                if s == 0:
                    gate_products(layer)
                if s == 1:
                    rotate(layer, 0, q[:, 0, :], 0, 0)
                    rotate(layer, 1, q[:, 1, :], 1, 0)
                if s == 2:
                    rotate(layer, 2, q[:, 2, :], 0, 1)
                    rotate(layer, 3, q[:, 3, :], 1, 1)
                if s == 3:
                    rotate(layer, 4, kT[:, :], 0, 2)
                if s == 4:
                    pe.wait_ge(proj.sem, proj.val(layer, proj_count(3)))
                    pe.wait_ge(rot_used.sem, rot_used.val(layer, 4))
                    for n in range(NB):
                        ins = T.transpose(sd[:, 1, P * n:P * n + P], vT[:, P * n:P * n + P], ident)
                    ins.then_inc(v_ps.sem, 1)
                if 6 <= s < 14:
                    u = s - 6
                    b = sx[u % 2]
                    pe.wait_ge(p_ready.sem, p_ready.val(layer, u + 1))
                    if u == 0:
                        pe.wait_ge(cols_ready.sem, cols_ready.val(layer, 1))
                    else:
                        pe.wait_ge(o_used.sem, o_used.val(layer, u))
                    for w in ((0, 1) if u >= 2 else (1,)):
                        for j in range(4):
                            ins = T.transpose(sd[:, 2 + w, P * j:P * j + P], b[:, j, P * w:P * w + P], ident)
                    ins.then_inc(pT_ps.sem, 1)
                if 5 <= s < 13:
                    u = s - 5
                    blk, g = divmod(u, 2)
                    if u == 0:
                        pe.wait_ge(roped.sem, roped.val(layer, 5))
                        pe.wait_ge(v_ready.sem, v_ready.val(layer, 1))
                    else:
                        pe.wait_ge(sc_max.sem, sc_max.val(layer, u))
                    half_ = slice(HD * g, HD * g + HD)
                    k0 = 1 if u < 2 else 0
                    for j in range(4):
                        ins = T.matmul(sd[:, j // 2, 256 * (j % 2) + P * k0:256 * (j % 2) + 256],
                                       q[half_, j, P * blk:P * blk + P], kT[half_, P * (blk - 1 + k0):P * (blk + 1)],
                                       start=True, stop=True)
                    ins.then_inc(sc_ps.sem, 1)
                if 18 <= s < 30 and (s - 18) % 3 == 0:
                    h = (s - 18) // 3
                    pe.wait_ge(s_ready.sem, s_ready.val(layer, h + 1))
                    pe.wait_ge(vt_ready.sem, vt_ready.val(layer, h + 1))
                    for n in range(NB):
                        T.matmul(sd[:, 1, P * n:P * n + P], Dm[:, n, :], vt[:, n, :], start=True, stop=True)
                        T.matmul(sd[:, 3, n:n + 1], Dm[:, n, :], ones[:, 0:1], start=True, stop=True)
                    for n in range(NB - 1):
                        T.matmul(sd[:, 2, P * n:P * n + P], kw[:, n, :], vt[:, n, :], start=True, stop=True)
                        ins = T.matmul(sd[:, 3, 8 + n:9 + n], kw[:, n, :], ones[:, 0:1], start=True, stop=True)
                    ins.then_inc(m2_ps.sem, 1)

            def mixer(layer):
                for s in range(S_MIX):
                    n = S_FFN + s
                    t, r = divmod(s - 18, 3)
                    mid = lambda: middle_job(layer, s)
                    pair = (2 * (s % 2), 2 * (s % 2) + 1)
                    if 2 <= s < 18:
                        pe.wait_ge(proj.sem, proj.val(layer, proj_count(s - 2)))
                    if s < 2:
                        slab(layer, n, pair, xhk, xlk, middle=mid,
                             before_k=stream_wait(layer, 1) if s == 0 else None)
                    elif s < 4:
                        slab(layer, n, pair[0:1], xhk, xlk, middle=mid)
                    elif s < 18:
                        slab(layer, n, pair, xhk, xlk, middle=mid)
                    elif s < 36 and r < 2:
                        if t == 0:
                            pe.wait_ge(proj.sem, proj.val(layer, proj_count(16 + r)))
                        else:
                            pe.wait_ge(prod.sem, prod.val(layer, 4 * (t - 1) + 2 * r + 2))
                        slab(layer, n, (2 * r, 2 * r + 1), xhk, xlk, middle=mid)
                    elif s < 36:
                        bh, bl, ready = ((yCh, yCl, yc_lo), (yAh, yAl, ya_lo), (yMh, yMl, ym_lo))[t // 2]
                        pe.wait_ge(ready.sem, ready.val(layer, 4))

                        def before(m):
                            if m == 2:
                                middle_job(layer, s)
                            pe.wait_ge(sig_ready.sem, sig_ready.val(layer, 4 * t + m + 1))

                        slab(layer, n, (0, 1, 2, 3), lambda k: bh[:, k, :], lambda k: bl[:, k, :], between=br_ps,
                             before_m=before)
                    else:
                        if s < 38:
                            pe.wait_ge(prod.sem, prod.val(layer, 20 + 2 * (s - 36) + 2))
                        elif s == 38:
                            pe.wait_ge(z_ready.sem, z_ready.val(layer, 2 * CENTRE))
                        else:
                            pe.wait_ge(d_ready.sem, d_ready.val(layer, KD + 4))
                        slab(layer, n, pair, lambda k: mh[k // 4][:, k % 4, :], lambda k: ml[k // 4][:, k % 4, :], middle=mid,
                             before_k=(lambda k: pe.wait_ge(mg_lo.sem, mg_lo.val(layer, k + 1))) if s == 36 else None,
                             between=seventh_ps if s == 39 else None)
                    end_job(layer, s)
                stat_sums(layer, 1)

            pe.sem_inc(slab_done.sem, 1)
            pe.sem_inc(gate_ps.sem, 1)
            with pe.Fori(0, DEPTH) as layer:
                ffn(layer, 0, 0)
                mixer(layer)
                ffn(layer, S_FFN + S_MIX, 1)


def proj_count(s):
    return 2 * (s + 1) if s < 2 else s + 3 if s < 4 else 6 + 2 * (s - 3)


SETUP_STEPS = 11


def params(b_in, attn_sinks, mlstm_norm_w, conv_w, ln_w, ln_b):
    out = np.zeros((DEPTH, P, NPAR), np.float32)
    for la in range(DEPTH):
        b = b_in[la]
        bq = b[C_AQ:C_AQ + 512].reshape(2, 4, HD)
        for j in range(4):
            out[la, :, B_Q + j] = np.concatenate([bq[0, j], bq[1, j]])
        for col, c, n in ((B_K, C_AK, 1), (B_V, C_AV, 1), (B_MQ, C_MQ, 16), (B_CX, C_CX, 4),
                          (B_CC, C_CX + 2 * WB, 4), (B_CB, C_CX + WB, 4), (B_G, C_GATE, 24)):
            out[la, :, col:col + n] = b[c:c + P * n].reshape(n, P).T
        for j in range(3):
            for w, t in enumerate((ln_w, ln_b)):
                c = PAR_LN + 16 * j + 8 * w
                out[la, :, c:c + 8] = t[la, j].reshape(KD, P).T
        out[la, :, PAR_NW:PAR_NW + 4] = mlstm_norm_w[la].reshape(MH, P).T
        for k in range(3):
            out[la, :, PAR_CONV + 4 * k:PAR_CONV + 4 * k + 4] = conv_w[la, k].reshape(4, P).T
        out[la, :, PAR_IF:PAR_IF + 8] = b[C_IF:C_IF + 8]
        out[la, :, PAR_SINK:PAR_SINK + 8] = attn_sinks[la]
    return out


def constants():
    c = np.zeros((P, NCONST), np.float32)
    i, j = np.arange(P)[:, None], np.arange(P)[None, :]
    c[:, K_ID:K_ID + P] = i == j
    c[:, K_ONE:K_ONE + P] = 1.0
    half = ROT // 2
    for h in (0, HD):
        for d in range(half):
            c[h + d + half, K_ROT + h + d] = -1.0
            c[h + d, K_ROT + h + d + half] = 1.0
            c[h + d, K_FREQ] = c[h + d + half, K_FREQ] = THETA ** (-2.0 * d / ROT)
    c[:, K_MASK:K_MASK + P] = np.where(j > i, 0.0, NEG)
    c[:, K_MASK + P:K_MASK + 2 * P] = np.where(j <= i, 0.0, NEG)
    c[:, K_MT:K_MT + P] = np.where(j >= i, 0.0, NEG)
    for h in range(MH):
        for n in range(NB):
            c[4 * n + h, K_HM + 4 * h + n] = 1.0
    return c


def kernel(x, positions, w_in, b_in, attn_sinks, mlstm_norm_w, conv_w, w_branch, w_out,
           ffn1_w_gu, ffn1_w_down, ffn2_w_gu, ffn2_w_down, ln_w, ln_b):
    import concourse.bacc as bacc
    from concourse.bass_utils import run_bass_kernel_spmd

    a = {k: np.asarray(v) for k, v in dict(
        b_in=b_in, attn_sinks=attn_sinks, mlstm_norm_w=mlstm_norm_w, conv_w=conv_w, ln_w=ln_w, ln_b=ln_b).items()}
    arrays = {
        "xT": np.ascontiguousarray(np.asarray(x)[0].T), "positions": np.asarray(positions),
        "w_in": np.asarray(w_in), "w_branch": np.asarray(w_branch), "w_out": np.asarray(w_out),
        "gu1": np.asarray(ffn1_w_gu), "down1": np.asarray(ffn1_w_down),
        "gu2": np.asarray(ffn2_w_gu), "down2": np.asarray(ffn2_w_down),
        "par": params(**a), "constants": constants(),
    }
    nc = bacc.Bacc("TRN2", target_bir_lowering=False, num_devices=1)
    args = [nc.dram_tensor(n, v.shape, mybir.dt.from_np(v.dtype), kind="ExternalInput").ap() for n, v in arrays.items()]
    outT = nc.dram_tensor("outT", (D, SEQ), F32, kind="ExternalOutput").ap()
    build(nc, *args, outT)
    r = run_bass_kernel_spmd(nc, [arrays], core_ids=[0])
    return np.ascontiguousarray(r.results[0]["outT"].T)[None]
```
